# Optimizing a Trainium2 kernel written in Bass

```python
import jax, jax.numpy as jnp
from jax import lax
import numpy as np

D_MODEL = 1024
BATCH = 1
SEQ = 256
DEPTH = 1
DEC_BATCH = 8
DEC_SEQ = 1
PAST_LEN = 2048
PAGE_SIZE = 128

N_META = 16
CONV_WIDTH = 31
D_CONV = D_MODEL
N_RET_HEADS = 4
RET_DK = D_MODEL // N_RET_HEADS
RET_DV = 2 * RET_DK
D_QK = N_RET_HEADS * RET_DK
D_V = N_RET_HEADS * RET_DV
CHUNK = 128
ROPE_BASE = 10000.0
N_GROUPS = 4
EXPERTS_PER_GROUP = 4
N_EXPERTS = N_GROUPS * EXPERTS_PER_GROUP
TOP_K_INNER = 2
D_EXPERT = D_MODEL // 2
EPS = 1e-6
D_IN = 2 * D_CONV + 2 * D_QK + 2 * D_V + 2 * D_MODEL

kernel_name = 'hybrid_conv_retention_hmoe_step'

def _rmsnorm(x, g):
    xf = x.astype(jnp.float32)
    y = xf * lax.rsqrt(jnp.mean(xf * xf, -1, keepdims=True) + EPS)
    return (y * g.astype(jnp.float32)).astype(x.dtype)

def _rotary(x, pos):
    half = x.shape[-1] // 2
    freqs = jnp.power(ROPE_BASE, -jnp.arange(half, dtype=jnp.float32) / half)
    ang = pos.astype(jnp.float32)[:, None] * freqs[None, :]
    cos = jnp.cos(ang)[None, :, None, :]
    sin = jnp.sin(ang)[None, :, None, :]
    xf = x.astype(jnp.float32)
    x1, x2 = xf[..., :half], xf[..., half:]
    return jnp.concatenate([x1 * cos - x2 * sin, x1 * sin + x2 * cos], -1)

def _ret_log_gamma():
    return jnp.log(1.0 - jnp.exp2(-5.0 - jnp.arange(N_RET_HEADS, dtype=jnp.float32)))

def _retention_chunk(q, k, v, S, lg):
    L = q.shape[1]
    idx = jnp.arange(L, dtype=jnp.float32)
    diff = idx[:, None] - idx[None, :]
    dmat = jnp.where((diff >= 0)[None], jnp.exp(jnp.maximum(diff, 0.0)[None] * lg[:, None, None]), 0.0)
    scores = jnp.einsum('bihd,bjhd->bhij', q, k) * dmat[None]
    o = jnp.einsum('bhij,bjhe->bihe', scores, v)
    q_dec = q * jnp.exp((idx[:, None] + 1.0) * lg[None, :])[None, :, :, None]
    o = o + jnp.einsum('bihd,bhde->bihe', q_dec, S)
    k_dec = k * jnp.exp((L - 1.0 - idx)[:, None] * lg[None, :])[None, :, :, None]
    S_new = jnp.exp(L * lg)[None, :, None, None] * S + jnp.einsum('bjhd,bjhe->bhde', k_dec, v)
    return o, S_new

def _retention(q, k, v, S0, n_lead):
    lg = _ret_log_gamma()
    outs = []
    S = S0
    if n_lead > 0:
        o, S = _retention_chunk(q[:, :n_lead], k[:, :n_lead], v[:, :n_lead], S, lg)
        outs.append(o)
        q, k, v = q[:, n_lead:], k[:, n_lead:], v[:, n_lead:]
    B, T = q.shape[0], q.shape[1]
    n_full = T // CHUNK
    if n_full > 0:
        Tf = n_full * CHUNK

        def to_chunks(a):
            return jnp.swapaxes(a[:, :Tf].reshape(B, n_full, CHUNK, *a.shape[2:]), 0, 1)

        def step(S, qkv):
            o, S = _retention_chunk(qkv[0], qkv[1], qkv[2], S, lg)
            return S, o

        S, o = lax.scan(step, S, (to_chunks(q), to_chunks(k), to_chunks(v)))
        outs.append(jnp.swapaxes(o, 0, 1).reshape(B, Tf, N_RET_HEADS, RET_DV))
        q, k, v = q[:, Tf:], k[:, Tf:], v[:, Tf:]
    if q.shape[1] > 0:
        o, S = _retention_chunk(q, k, v, S, lg)
        outs.append(o)
    return jnp.concatenate(outs, 1), S

def _mixer(h, S0, buf0, pos, n_lead, w_in, b_gates, conv_w, conv_b, conv_ln_g, conv_ln_b,
           w_conv_out, ret_gn_g, w_ret_out, w_o):
    B, T, _ = h.shape
    proj = h @ w_in
    sizes = [D_CONV, D_CONV, D_QK, D_QK, D_V, D_V, D_MODEL, D_MODEL]
    offs, acc = [], 0
    for s in sizes[:-1]:
        acc += s
        offs.append(acc)
    glu_a, glu_b, q, k, v, g_ret, gate_a, gate_b = jnp.split(proj, offs, axis=-1)

    u = glu_a * jax.nn.sigmoid(glu_b)
    ext = jnp.concatenate([buf0.astype(u.dtype), u], axis=1)
    buf_new = ext[:, ext.shape[1] - (CONV_WIDTH - 1):]
    c = lax.conv_general_dilated(ext, conv_w[:, None, :].astype(ext.dtype), window_strides=(1,),
                                 padding='VALID', dimension_numbers=('NWC', 'WIO', 'NWC'),
                                 feature_group_count=D_CONV) + conv_b
    cf = c.astype(jnp.float32)
    mu = jnp.mean(cf, -1, keepdims=True)
    var = jnp.mean(jnp.square(cf - mu), -1, keepdims=True)
    cn = (cf - mu) * lax.rsqrt(var + EPS) * conv_ln_g.astype(jnp.float32) + conv_ln_b.astype(jnp.float32)
    y_a = jax.nn.silu(cn).astype(h.dtype) @ w_conv_out

    qh = _rotary(q.reshape(B, T, N_RET_HEADS, RET_DK), pos)
    kh = _rotary(k.reshape(B, T, N_RET_HEADS, RET_DK), pos) * (RET_DK ** -0.5)
    vh = v.reshape(B, T, N_RET_HEADS, RET_DV).astype(jnp.float32)
    o, S_new = _retention(qh, kh, vh, S0.astype(jnp.float32), n_lead)
    omu = jnp.mean(o, -1, keepdims=True)
    ovar = jnp.mean(jnp.square(o - omu), -1, keepdims=True)
    on = ((o - omu) * lax.rsqrt(ovar + EPS)).reshape(B, T, D_V) * ret_gn_g.astype(jnp.float32)
    y_b = (on * jax.nn.silu(g_ret.astype(jnp.float32))).astype(h.dtype) @ w_ret_out

    g_a = jax.nn.sigmoid(gate_a + b_gates[:D_MODEL])
    g_b = jax.nn.sigmoid(gate_b + b_gates[D_MODEL:])
    out = (g_a * y_a + g_b * y_b) @ w_o
    return out.astype(h.dtype), S_new.astype(S0.dtype), buf_new.astype(buf0.dtype)

def _hier_moe(h, w_coarse, b_coarse, w_fine, b_fine, w_gate_e, w_up_e, w_down_e):
    B, T, D = h.shape
    t = h.reshape(B * T, D)
    cprob = jax.nn.softmax((t @ w_coarse + b_coarse).astype(jnp.float32), axis=-1)
    g_sel = jnp.argmax(cprob, axis=-1)
    p_g = jnp.take_along_axis(cprob, g_sel[:, None], axis=1)[:, 0]
    fl = (t @ w_fine + b_fine).astype(jnp.float32).reshape(B * T, N_GROUPS, EXPERTS_PER_GROUP)
    sel = jnp.take_along_axis(fl, g_sel[:, None, None], axis=1)[:, 0]
    vals, idx = lax.top_k(sel, TOP_K_INNER)
    w = jax.nn.softmax(vals, axis=-1)
    eid = g_sel[:, None] * EXPERTS_PER_GROUP + idx
    comb = p_g[:, None] * jnp.sum(w[..., None] * jax.nn.one_hot(eid, N_EXPERTS, dtype=jnp.float32), axis=1)
    hg = jnp.einsum('nd,edf->nef', t, w_gate_e)
    hu = jnp.einsum('nd,edf->nef', t, w_up_e)
    act = jax.nn.silu(hg) * hu * comb[:, :, None].astype(hg.dtype)
    out = jnp.einsum('nef,efd->nd', act, w_down_e)
    return out.reshape(B, T, D).astype(h.dtype)

def _layer(x, S0, buf0, pos, n_lead, norm_mix_g, w_in, b_gates, conv_w, conv_b, conv_ln_g, conv_ln_b,
           w_conv_out, ret_gn_g, w_ret_out, w_o, norm_ffn_g, w_coarse, b_coarse, w_fine, b_fine,
           w_gate_e, w_up_e, w_down_e):
    h = _rmsnorm(x, norm_mix_g)
    mix, S_new, buf_new = _mixer(h, S0, buf0, pos, n_lead, w_in, b_gates, conv_w, conv_b, conv_ln_g,
                                 conv_ln_b, w_conv_out, ret_gn_g, w_ret_out, w_o)
    x = x + mix
    x = x + _hier_moe(_rmsnorm(x, norm_ffn_g), w_coarse, b_coarse, w_fine, b_fine, w_gate_e, w_up_e, w_down_e)
    return x, S_new, buf_new

def setup_inputs(seed: int = 0) -> dict:
    key = jax.random.key(seed)
    ks = jax.random.split(key, 32)

    def nrm(k, shape, scale):
        return jax.random.normal(k, shape, jnp.float32) * scale

    L = DEPTH
    return {
        'x_prompt': nrm(ks[0], (BATCH, SEQ, D_MODEL), 1.0),
        'x_sample': nrm(ks[1], (DEC_BATCH, DEC_SEQ, D_MODEL), 1.0),
        'state_ret': nrm(ks[2], (L, DEC_BATCH, N_RET_HEADS, RET_DK, RET_DV), 0.5),
        'state_conv': nrm(ks[3], (L, DEC_BATCH, CONV_WIDTH - 1, D_CONV), 0.5),
        'meta_tokens': nrm(ks[4], (N_META, D_MODEL), 1.0),
        'norm_mix_g': 1.0 + nrm(ks[5], (L, D_MODEL), 0.02),
        'w_in': nrm(ks[6], (L, D_MODEL, D_IN), D_MODEL ** -0.5),
        'b_gates': nrm(ks[7], (L, 2 * D_MODEL), 0.02),
        'conv_w': nrm(ks[8], (L, CONV_WIDTH, D_CONV), CONV_WIDTH ** -0.5),
        'conv_b': nrm(ks[9], (L, D_CONV), 0.02),
        'conv_ln_g': 1.0 + nrm(ks[10], (L, D_CONV), 0.02),
        'conv_ln_b': nrm(ks[11], (L, D_CONV), 0.02),
        'w_conv_out': nrm(ks[12], (L, D_CONV, D_MODEL), D_CONV ** -0.5),
        'ret_gn_g': 1.0 + nrm(ks[13], (L, D_V), 0.02),
        'w_ret_out': nrm(ks[14], (L, D_V, D_MODEL), D_V ** -0.5),
        'w_o': nrm(ks[15], (L, D_MODEL, D_MODEL), D_MODEL ** -0.5),
        'norm_ffn_g': 1.0 + nrm(ks[16], (L, D_MODEL), 0.02),
        'w_coarse': nrm(ks[17], (L, D_MODEL, N_GROUPS), D_MODEL ** -0.5),
        'b_coarse': nrm(ks[18], (L, N_GROUPS), 0.01),
        'w_fine': nrm(ks[19], (L, D_MODEL, N_EXPERTS), D_MODEL ** -0.5),
        'b_fine': nrm(ks[20], (L, N_EXPERTS), 0.01),
        'w_gate_e': nrm(ks[21], (L, N_EXPERTS, D_MODEL, D_EXPERT), D_MODEL ** -0.5),
        'w_up_e': nrm(ks[22], (L, N_EXPERTS, D_MODEL, D_EXPERT), D_MODEL ** -0.5),
        'w_down_e': nrm(ks[23], (L, N_EXPERTS, D_EXPERT, D_MODEL), D_EXPERT ** -0.5),
        'norm_final_g': 1.0 + nrm(ks[24], (D_MODEL,), 0.02),
    }

def reference(x_prompt, x_sample, state_ret, state_conv, meta_tokens, norm_mix_g, w_in, b_gates, conv_w,
              conv_b, conv_ln_g, conv_ln_b, w_conv_out, ret_gn_g, w_ret_out, w_o, norm_ffn_g, w_coarse,
              b_coarse, w_fine, b_fine, w_gate_e, w_up_e, w_down_e, norm_final_g):
    Bp = x_prompt.shape[0]
    meta = jnp.broadcast_to(meta_tokens[None].astype(x_prompt.dtype), (Bp, N_META, D_MODEL))
    yp = jnp.concatenate([meta, x_prompt], axis=1)
    pos_p = jnp.arange(yp.shape[1], dtype=jnp.float32)
    pos_s = PAST_LEN + jnp.arange(x_sample.shape[1], dtype=jnp.float32)
    ys = x_sample
    zero_S = jnp.zeros((Bp, N_RET_HEADS, RET_DK, RET_DV), state_ret.dtype)
    zero_buf = jnp.zeros((Bp, CONV_WIDTH - 1, D_CONV), state_conv.dtype)
    sp, bp, ss, bs = [], [], [], []
    for l in range(DEPTH):
        lp = (norm_mix_g[l], w_in[l], b_gates[l], conv_w[l], conv_b[l], conv_ln_g[l], conv_ln_b[l],
              w_conv_out[l], ret_gn_g[l], w_ret_out[l], w_o[l], norm_ffn_g[l], w_coarse[l], b_coarse[l],
              w_fine[l], b_fine[l], w_gate_e[l], w_up_e[l], w_down_e[l])
        yp, s1, b1 = _layer(yp, zero_S, zero_buf, pos_p, N_META, *lp)
        ys, s2, b2 = _layer(ys, state_ret[l], state_conv[l], pos_s, 0, *lp)
        sp.append(s1)
        bp.append(b1)
        ss.append(s2)
        bs.append(b2)
    y_prompt = _rmsnorm(yp, norm_final_g)[:, N_META:]
    y_sample = _rmsnorm(ys, norm_final_g)
    new_state_ret_prompt = jnp.stack(sp, 0)
    new_state_conv_prompt = jnp.stack(bp, 0)
    new_state_ret_sample = jnp.stack(ss, 0)
    new_state_conv_sample = jnp.stack(bs, 0)
    return (y_prompt, y_sample, new_state_ret_prompt, new_state_conv_prompt, new_state_ret_sample, new_state_conv_sample)


_drawn_inputs = setup_inputs


def setup_inputs(seed=0):
    import zlib

    import numpy as np

    out = dict(_drawn_inputs(seed))
    spreads = {}
    factors = {'b_gates': 8.0,
     'conv_ln_g': 19.187,
     'conv_ln_b': 18.75,
     'ret_gn_g': 21.54,
     'b_coarse': 22.365,
     'b_fine': 31.529,
     'norm_final_g': 7.822,
     'norm_ffn_g': 5.113}
    for name, (base, spread) in spreads.items():
        noise = np.random.default_rng([zlib.crc32(name.encode()), seed]).standard_normal(out[name].shape)
        drawn = base * np.exp(spread * noise) if base else spread * noise
        out[name] = __import__('jax').numpy.asarray(drawn.astype(out[name].dtype))
    for name, factor in factors.items():
        out[name] = (out[name] * factor).astype(out[name].dtype)
    return out
```

```python
import concourse.bass as bass
from concourse import mybir
from contextlib import ExitStack
import numpy as np

D = 1024
KT = D // 128
SEQ, NMETA, NSAMP = 256, 16, 8
TP = NMETA + SEQ
T = TP + NSAMP
TOKENS = [(0, 128), (128, 128), (256, T - 256)]
NH, DK, DV = 4, 256, 512
ET = NH * DV // 128
CW = 31
PAD = CW - 1
UW = PAD + T
NE, NG, DE = 16, 4, 512
PAST = 2048
EPS = 1e-6
GAMMA = [1.0 - 2.0 ** (-5 - h) for h in range(NH)]
BANKS = 7
WS = 3

PAR = {}
_n = 0
for _name, _k in (("norm_mix", 8), ("b_gates", 16), ("conv_b", 8), ("ln_g", 8), ("ln_b", 8), ("gn_g", 16),
                  ("norm_ffn", 8), ("norm_final", 8)):
    PAR[_name] = _n
    _n += _k
NPAR = _n

CON = {}
_n = 0
for _name, _k in (("ident", 128), ("cos", T), ("sin", T), ("mask", NH * TP), ("kdecay", 3 * NH), ("mean_d", 128),
                  ("mean_v", 128), ("eps", 1), ("rank", 4)):
    CON[_name] = (_n, _k)
    _n += _k
NCON = _n


def constants():
    c = np.zeros((128, NCON), np.float32)

    def put(name, a):
        at, k = CON[name]
        c[:, at:at + k] = a

    half = DK // 2
    pos = np.concatenate([np.arange(TP), np.full(NSAMP, PAST)]).astype(np.float32)
    freq = np.power(np.float32(10000.0), -np.arange(half, dtype=np.float32) / np.float32(half)).astype(np.float32)
    ang = (freq[:, None] * pos[None, :]).astype(np.float32).astype(np.float64)
    put("ident", np.eye(128))
    put("cos", np.cos(ang))
    put("sin", np.sin(ang))
    i, j = np.arange(TP)[None, :], np.arange(128)[:, None]
    put("mask", np.concatenate([np.where(i >= j, g ** np.maximum(i - j, 0), 0.0) for g in map(float, GAMMA)], 1))
    kd = np.zeros((128, 3, NH))
    for tt, (t0, n) in enumerate(TOKENS):
        for p in range(min(n, TP - t0)):
            kd[p, tt] = [g ** (TP - 1 - t0 - p) for g in GAMMA]
    put("kdecay", kd.reshape(128, 3 * NH))
    put("mean_d", np.full((128, 128), 1.0 / D))
    put("mean_v", np.full((128, 128), 1.0 / DV))
    put("eps", np.full((128, 1), EPS))
    put("rank", np.tile(np.arange(4, 0, -1), (128, 1)))
    return c


UNITS = []
for _s, _c in (("q", 8), ("k", 8), ("v", 16)):
    UNITS += [(_s, i) for i in range(_c)]
for _j in range(4):
    UNITS += [("glu_b", 2 * _j), ("glu_b", 2 * _j + 1), ("glu_a", 2 * _j), ("glu_a", 2 * _j + 1)]
UNITS += [("gret", i) for i in range(16)] + [("ret", i) for i in range(16)]
UNITS += [("gate_b", i) for i in range(8)] + [("gate_a", i) for i in range(8)]
UNITS += [("cout", i) for i in range(8)] + [("wo", i) for i in range(8)]
NMIX = len(UNITS)
for _e in range(NE):
    for _f in (0, 2):
        UNITS += [("g", _e, _f), ("g", _e, _f + 1), ("u", _e, _f), ("u", _e, _f + 1)]
    UNITS += [("d", _e, i) for i in range(4)]
FIRST = {}
for _w, _u in enumerate(UNITS):
    FIRST.setdefault(_u[0], _w)
GLU, GRET = FIRST["glu_b"], FIRST["gret"]
EXTRA_END = GRET + 16

TILES = []
UNIT_TILE = {}


def _tiles():
    add = TILES.append
    add((("par",), "D"))
    for tt in range(3):
        for hf in range(2):
            add((("xt", tt, hf), "D" if hf else "A"))
    add((("norm", 0), "A"))
    for w in range(NMIX):
        u = UNITS[w]
        s, i = u
        if s == "ret":
            if i % 2:
                add((("m", w), "A"))
        elif s in ("q", "k", "v", "glu_b"):
            add((("m", w), "A"))
        elif s == "gate_b" or s == "glu_a" or s in ("gret", "cout", "wo"):
            add((("m", w), "D"))
        elif s == "gate_a":
            add((("m", w), "A"))
        if w == 1:
            add((("cw",), "D"))
        if 2 <= w < 6:
            add((("sc", (w - 2) // 2, w % 2), "A"))
        if FIRST["v"] < w <= FIRST["v"] + 16:
            add((("vt", w - 1 - FIRST["v"]), "D"))
        if GLU <= w < EXTRA_END:
            k = w - GLU
            if k < NH:
                add((("score", k), "D"))
                add((("kt", k, 0), "A"))
                add((("kt", k, 1), "A"))
            if 1 <= k <= NH:
                for et in range(4):
                    add((("o", k - 1, et), "A"))
                for dt in range(2):
                    add((("S", k - 1, dt), "A"))
            if k < 16:
                add((("vb", k, 0), "D"))
                add((("vb", k, 1), "D"))
            if k >= 5 and (k - 5) % 4 == 0 and k <= 17:
                add((("ot", (k - 5) // 4), "A"))
            if k >= 6 and (k - 6) % 4 == 0 and k <= 18:
                add((("gm", (k - 6) // 4), "D"))
            if k >= 7 and (k - 7) % 4 == 0 and k <= 19:
                add((("gv", (k - 7) // 4), "A"))
            if k in (20, 21):
                add((("ut", k - 20), "A"))
        if w == FIRST["cout"] - 4:
            add((("lm",), "D"))
        if w == FIRST["cout"] - 3:
            add((("lv",), "A"))
    add((("norm", 1), "A"))
    add((("logit",), "A"))
    add((("lt",), "D"))
    for e in range(NE):
        add((("cb", e), "A"))
    for w in range(NMIX, len(UNITS)):
        u = UNITS[w]
        if u[0] == "g":
            add((("m", w), "D"))
        elif u[0] == "u":
            add((("m", w), "D"))
        else:
            add((("m", w, 0), "D"))
            add((("m", w, 1), "D"))
    add((("norm", 2), "A"))
    for tt in range(3):
        for hf in range(2):
            add((("yt", tt, hf), "D" if hf else "A"))


_tiles()
TILE = {}
_cnt = {"A": 0, "D": 0}
for _i, (_name, _f) in enumerate(TILES):
    _cnt[_f] += 1
    TILE[_name] = (_i, _f, _cnt[_f])
for _w, _u in enumerate(UNITS):
    if _w < NMIX and _u[0] == "ret":
        UNIT_TILE[_w] = TILE[("m", _w | 1)][0]
    elif _w < NMIX or _u[0] != "d":
        UNIT_TILE[_w] = TILE[("m", _w)][0]
    else:
        UNIT_TILE[_w] = TILE[("m", _w, 1)][0]


def build(nc, A, C, O):
    f32, f32r = mybir.dt.float32, mybir.dt.float32r
    ALU, ACT, AX = mybir.AluOpType, mybir.ActivationFunctionType, mybir.AxisListType

    ctx = ExitStack()
    with ctx:
        def sb(name, shape, dt=f32):
            return ctx.enter_context(nc.sbuf_tensor(name, shape, dt))

        def overlay(name, *sets):
            out, most = {}, 0
            for s in sets:
                size = 0
                with ExitStack() as inner:
                    for n, shape, dt in s:
                        out[n] = inner.enter_context(nc.sbuf_tensor(n, shape, dt))
                        size += -(-int(np.prod(shape[1:])) * 4 // 32) * 32
                most = max(most, size)
            sb(name, [128, most // 4])
            return out

        def sem(name):
            return ctx.enter_context(nc.semaphore(name))

        con = sb("con", [128, NCON])
        par_rows = sb("par_rows", [NPAR, 128])
        par = sb("par", [128, NPAR])
        cw = sb("cw", [128, KT, CW])
        wr = sb("wr", [128, KT, 20])
        br = sb("br", [20, 1])
        xT = sb("xT", [128, KT, T])
        h_hi = sb("h_hi", [128, KT, T], f32r)
        h_lo = sb("h_lo", [128, KT, T], f32r)
        raw = [sb(f"raw{i}", [128, 2048]) for i in range(WS)]
        w_hi = [sb(f"w_hi{i}", [128, 1024], f32r) for i in range(WS)]
        w_lo = [sb(f"w_lo{i}", [128, 1024], f32r) for i in range(WS)]
        sg = sb("sg", [128, 2, T])
        rstd = sb("rstd", [128, T])
        mixer = [("v_tok", [128, 3, NH * DV], f32), ("k_tok", [128, 2, 3, DK], f32), ("P", [128, 432], f32), ("osb", [NSAMP, DV], f32)]
        with ExitStack() as mx:
            def mo(sets):
                out, most = {}, 0
                for s in sets:
                    size = 0
                    with ExitStack() as inner:
                        for n, shape, dt in s:
                            out[n] = inner.enter_context(nc.sbuf_tensor(n, shape, dt))
                            size += -(-int(np.prod(shape[1:])) * 4 // 32) * 32
                    most = max(most, size)
                mx.enter_context(nc.sbuf_tensor(f"hold_{s[0][0]}", [128, most // 4], f32))
                return out

            R1 = mo([mixer, [("x_tok", [128, 3, D], f32), ("sc_rows", [120, 2, D], f32)],
                     [("on_hi", [128, ET, T], f32r), ("on_lo", [128, ET, T], f32r)],
                     [("m_hi", [128, KT, T], f32r), ("m_lo", [128, KT, T], f32r)]])
            R2 = mo([[("oT", [128, ET, T], f32)], [("stT", [128, KT, 240], f32), ("cw_rows", [CW, D], f32)],
                     [("yb", [128, KT, T], f32), ("ga", [128, KT, T], f32)]])
            R3 = mo([[("qT", [128, KT, T], f32), ("kT", [128, KT, T], f32)],
                     [("dummy_q", [128, KT, T], f32), ("sq0", [128, KT, T], f32)],
                     [("c_hi", [128, KT, T], f32r), ("c_lo", [128, KT, T], f32r)]])
            R4 = mo([[("conv", [128, KT, T], f32)], [("hf", [128, KT, T], f32)]])
            R5 = mo([[("S_ring", [128, 2, 2, 2, DV], f32)], [("ln_sq", [128, KT, T], f32)]])
            u = mx.enter_context(nc.sbuf_tensor("u", [128, KT, UW], f32))
            csamp = mx.enter_context(nc.sbuf_tensor("csamp", [128, KT, NSAMP], f32))
            R6 = mo([[("qk", [128, 2, 2, T], f32)], [("gsq", [128, 4, T], f32)]])
            R7 = mo([[("rot", [128, 2, 2, T], f32)], [("tg", [128, 2, T], f32), ("gstd", [128, T], f32)]])
            R8 = mo([[("vT", [128, 2, T], f32)], [("S_out", [128, 2, DV], f32)]])
            vT, S_out = R8["vT"], R8["S_out"]
            qm = mx.enter_context(nc.sbuf_tensor("qm", [128, KT, NSAMP, NSAMP], f32))
            utok = S_out
        with ExitStack() as me:
            def mt(name, shape, dt=f32):
                return me.enter_context(nc.sbuf_tensor(name, shape, dt))
            comb_b = mt("comb_b", [128, NE, T])
            h2f = mt("h2f", [128, KT, T])
            sq1 = mt("sq1", [128, KT, T])
            a_f = mt("a_f", [128, 2, T])
            t_f = mt("t_f", [128, 2, T])
            a_hi = mt("a_hi", [128, 2, 4, T], f32r)
            a_lo = mt("a_lo", [128, 2, 4, T], f32r)
            lgT = mt("lgT", [20, T])
            lg = mt("lg", [128, 3, 20])
            rt = mt("rt", [128, 3, 160])
            comb = mt("comb", [128, 3, NE])
            y_tok = mt("y_tok", [128, 3, D])
        v_tok, k_tok, P, osb = R1["v_tok"], R1["k_tok"], R1["P"], R1["osb"]
        x_tok, sc_rows = R1["x_tok"], R1["sc_rows"]
        on_hi, on_lo, m_hi, m_lo = R1["on_hi"], R1["on_lo"], R1["m_hi"], R1["m_lo"]
        oT, stT, cw_rows, yb, ga = R2["oT"], R2["stT"], R2["cw_rows"], R2["yb"], R2["ga"]
        qT, kT, sq0, c_hi, c_lo = R3["qT"], R3["kT"], R3["sq0"], R3["c_hi"], R3["c_lo"]
        conv, hf, S_ring, ln_sq = R4["conv"], R4["hf"], R5["S_ring"], R5["ln_sq"]
        qk, gsq, rot, tg, gstd = R6["qk"], R6["gsq"], R7["rot"], R7["tg"], R7["gstd"]

        banks = [ctx.enter_context(nc.psum_tensor(f"bank{i}", [128, 512], f32)) for i in range(8)]
        o_samp = banks[7]

        def cst(name):
            at, k = CON[name]
            return con[:, at:at + k]

        ident = cst("ident")
        mask = cst("mask").rearrange("p (h i) -> p h i", h=NH)
        kdecay = cst("kdecay").rearrange("p (t h) -> p t h", t=3)
        eps = cst("eps")

        x_in, con_in, par_in, sc_in, cw_in, wr_in = (sem(n) for n in ("x_in", "con_in", "par_in", "sc_in", "cw_in", "wr_in"))
        raw_in = [sem(f"raw_in{i}") for i in range(WS)]
        S_in = [sem(f"S_in{i}") for i in range(2)]
        S_stored = [sem(f"S_stored{i}") for i in range(2)]
        Sp_stored = [sem(f"Sp_stored{i}") for i in range(2)]
        rows_stored, y_stored = sem("rows_stored"), sem("y_stored")
        hi_ready, lo_ready = sem("hi_ready"), sem("lo_ready")
        tile_ready = sem("tile_ready")
        act_freed, dve_freed = sem("act_freed"), sem("dve_freed")
        act_chain, dve_chain = sem("act_chain"), sem("dve_chain")
        S_used, S_scaled, S_new = sem("S_used"), sem("S_scaled"), sem("S_new")
        sig_ready, sq_ready, h_ready, hhi_ready, hlo_ready = (sem(n) for n in ("sig_ready", "sq_ready", "h_ready", "hhi_ready", "hlo_ready"))
        qk_ready, qm_ready, oc_ready, osq_ready, std_ready = (sem(n) for n in ("qk_ready", "qm_ready", "oc_ready", "osq_ready", "std_ready"))
        y_ready, yhi_ready, ylo_ready = sem("y_ready"), sem("yhi_ready"), sem("ylo_ready")
        m_ready, mhi_ready, mlo_ready = sem("m_ready"), sem("mhi_ready"), sem("mlo_ready")
        cc_ready, csq_ready, cz_ready, chi_ready, clo_ready, csig_ready = (sem(n) for n in ("cc_ready", "csq_ready", "cz_ready", "chi_ready", "clo_ready", "csig_ready"))
        conv_step, osb_ready, rot_ready, x2_ready = sem("conv_step"), sem("osb_ready"), sem("rot_ready"), sem("x2_ready")
        ex_ready, d_ready, comb_ready, ahi_ready, alo_ready, a_ready, y_done = (sem(n) for n in ("ex_ready", "d_ready", "comb_ready", "ahi_ready", "alo_ready", "a_ready", "y_done"))
        n_std = sem("n_std")

        def bank(name):
            return banks[TILE[name][0] % BANKS]

        def seen(e, name):
            e.wait_ge(tile_ready, TILE[name][0] + 1)

        def evacuated(e, name):
            _, f, k = TILE[name]
            e.wait_ge(act_freed if f == "A" else dve_freed, k)

        def unit_used(e, w):
            e.wait_ge(tile_ready, UNIT_TILE[w] + 1)

        def raw_view(w):
            s, m, r = UNITS[w][0], w % 2, raw[(w // 2) % WS]
            if s == "ret":
                return r[:, m * 1024:(m + 1) * 1024].rearrange("p (k n) -> p k n", k=8)
            if s == "d":
                return r[:, :].rearrange("p (k n) -> p k n", k=4)[:, :, m * 256:(m + 1) * 256]
            return r[:, :].rearrange("p (k n) -> p k n", k=8)[:, :, m * 128:(m + 1) * 128]

        def part_view(ring, w):
            return ring[w % WS][:, :].rearrange("p (k n) -> p k n", k=4 if UNITS[w][0] == "d" else 8)

        def weights_of(c):
            un = UNITS[2 * c]
            s = un[0]
            cols = {"q": 2048, "k": 3072, "v": 4096, "glu_a": 0, "glu_b": 1024, "gret": 6144, "gate_a": 8192, "gate_b": 9216}
            if s in cols:
                at = cols[s] + un[1] * 128
                return A["w_in"][0].rearrange("(k p) n -> p k n", p=128)[:, :, at:at + 256], 8
            if s == "ret":
                at = un[1] // 2 * 128
                return A["w_ret_out"][0].rearrange("(k p) n -> p k n", p=128)[:, :, at:at + 128], 16
            if s in ("cout", "wo"):
                at = un[1] * 128
                return A["w_conv_out" if s == "cout" else "w_o"][0].rearrange("(k p) n -> p k n", p=128)[:, :, at:at + 256], 8
            if s in ("g", "u"):
                at = un[2] * 128
                return A["w_gate_e" if s == "g" else "w_up_e"][0, un[1]].rearrange("(k p) n -> p k n", p=128)[:, :, at:at + 256], 8
            at = un[2] * 256
            return A["w_down_e"][0, un[1]].rearrange("(k p) n -> p k n", p=128)[:, :, at:at + 512], 4

        def conv_quota(w):
            if GLU + 4 <= w < GRET:
                return 6
            if GRET <= w < GRET + 16:
                return 3
            if GRET + 16 <= w < GRET + 32:
                return 5
            if GRET + 32 <= w < FIRST["cout"] - 4:
                return 12
            return 0

        block = ctx.enter_context(nc.Block())

        @block.sync
        def _(sp):
            xs, meta = A["x_prompt"][0], A["meta_tokens"]
            n1 = 128 - NMETA
            sp.dma_start(x_tok[0:NMETA, 0, :], meta).then_inc(x_in, 16)
            sp.dma_start(x_tok[NMETA:128, 0, :], xs[0:n1]).then_inc(x_in, 16)
            sp.dma_start(x_tok[:, 1, :], xs[n1:n1 + 128]).then_inc(x_in, 16)
            sp.dma_start(x_tok[0:16, 2, :], xs[n1 + 128:SEQ]).then_inc(x_in, 16)
            sp.dma_start(x_tok[16:24, 2, :], A["x_sample"][:, 0, :]).then_inc(x_in, 16)
            for c in range(len(UNITS) // 2):
                if c >= WS:
                    sp.wait_ge(lo_ready, 2 * (c - WS) + 2)
                src, k = weights_of(c)
                sp.dma_start(raw[c % WS][:, :].rearrange("p (k n) -> p k n", k=k), src).then_inc(raw_in[c % WS], 16)
            evacuated(sp, ("yt", 2, 1))
            evacuated(sp, ("yt", 2, 0))
            sp.dma_start(O["y_prompt"][0, 0:n1], y_tok[NMETA:128, 0, :]).then_inc(y_stored, 16)
            sp.dma_start(O["y_prompt"][0, n1:n1 + 128], y_tok[:, 1, :]).then_inc(y_stored, 16)
            sp.dma_start(O["y_prompt"][0, n1 + 128:SEQ], y_tok[0:16, 2, :]).then_inc(y_stored, 16)
            sp.dma_start(O["y_sample"][:, 0, :], y_tok[16:24, 2, :]).then_inc(y_stored, 16)
            sp.wait_ge(y_stored, 16 * 4)
            sp.wait_ge(rows_stored, 16 * 3)
            sp.wait_ge(S_stored[0], 16 * 8)
            sp.wait_ge(S_stored[1], 16 * 8)
            for i in range(2):
                sp.wait_ge(Sp_stored[i], 16 * NH)

        @block.gpsimd
        def _(pool):
            pool.dma_start(con[:, :], C).then_inc(con_in, 16)
            at = 0
            for name in ("norm_mix_g", "b_gates", "conv_b", "conv_ln_g", "conv_ln_b", "ret_gn_g", "norm_ffn_g"):
                v = A[name][0].rearrange("(k p) -> k p", p=128)
                pool.dma_start(par_rows[at:at + v.shape[0], :], v).then_inc(par_in, 16)
                at += v.shape[0]
            pool.dma_start(par_rows[at:at + 8, :], A["norm_final_g"].rearrange("(k p) -> k p", p=128)).then_inc(par_in, 16)
            pool.dma_start(cw_rows[:, :], A["conv_w"][0]).then_inc(cw_in, 16)
            sc = A["state_conv"][0].rearrange("(r b) t d -> (b t) r d", r=2)
            for r in range(2):
                pool.dma_start(sc_rows[:, r, :], A["state_conv"][0, 4 * r:4 * r + 4].rearrange("b t d -> (b t) d")).then_inc(sc_in, 16)
            pool.dma_start(wr[:, :, 0:4], A["w_coarse"][0].rearrange("(k p) n -> p k n", p=128)).then_inc(wr_in, 16)
            pool.dma_start(wr[:, :, 4:20], A["w_fine"][0].rearrange("(k p) n -> p k n", p=128)).then_inc(wr_in, 16)
            pool.dma_start(br[0:4, :], A["b_coarse"][0].rearrange("(n a) -> n a", a=1)).then_inc(wr_in, 16)
            pool.dma_start(br[4:20, :], A["b_fine"][0].rearrange("(n a) -> n a", a=1)).then_inc(wr_in, 16)
            pool.dma_start(O["conv_sample"][0, :, 0:CW - 2, :], A["state_conv"][0, :, 1:CW - 1, :]).then_inc(rows_stored, 16)

            def load(s):
                h, b = s // 4, s % 4 * 2
                src = A["state_ret"][0, b:b + 2, h].rearrange("b (t p) e -> p b t e", p=128)
                for i in range(2):
                    pool.dma_start(S_ring[:, s % 2, i], src[:, i]).then_inc(S_in[s % 2], 16)

            def store(s):
                h, b = s // 4, s % 4 * 2
                dst = O["ret_sample"][0, b:b + 2, h].rearrange("b (t p) e -> p b t e", p=128)
                evacuated(pool, ("vb", s, 1))
                for i in range(2):
                    pool.dma_start(dst[:, i], S_ring[:, s % 2, i]).then_inc(S_stored[s % 2], 16)

            load(0)
            load(1)
            for s in range(16):
                if s >= 1 and s <= NH:
                    h = s - 1
                    for dt in range(2):
                        evacuated(pool, ("S", h, dt))
                        pool.dma_start(O["ret_prompt"][0, 0, h, dt * 128:(dt + 1) * 128, :], S_out[:, dt, :]).then_inc(Sp_stored[dt], 16)
                store(s)
                if s + 2 < 16:
                    pool.wait_ge(S_stored[s % 2], 32 * (s // 2 + 1))
                    pool.wait_ge(S_used, s + 1)
                    load(s + 2)
            evacuated(pool, ("ut", 1))
            ut = utok[0:PAD + NSAMP, :, :].rearrange("p a b -> p (a b)")
            pool.dma_start(O["conv_prompt"][0, 0], ut[0:PAD, :]).then_inc(rows_stored, 16)
            pool.dma_start(O["conv_sample"][0, :, CW - 2, :], ut[PAD:PAD + NSAMP, :]).then_inc(rows_stored, 16)

        @block.scalar
        def _(act):
            n = {"chain": 0}

            def link(ins):
                n["chain"] += 1
                ins.then_inc(act_chain, 1)
                act.wait_ge(act_chain, n["chain"])

            def hi(w):
                if w >= len(UNITS):
                    return
                if w % 2 == 0:
                    act.wait_ge(raw_in[(w // 2) % WS], 16 * (w // 2 // WS + 1))
                if w >= WS:
                    unit_used(act, w - WS)
                act.activation(part_view(w_hi, w), raw_view(w), ACT.Copy).then_inc(hi_ready, 1)

            def free(ins):
                ins.then_inc(act_freed, 1)

            for tt, (t0, nt) in enumerate(TOKENS):
                seen(act, ("xt", tt, 0))
                src = bank(("xt", tt, 0))[:, :].rearrange("p (f n) -> p f n", f=4)[:, :, 0:nt]
                free(act.activation(xT[:, 0:4, t0:t0 + nt], src, ACT.Copy))
            evacuated(act, ("xt", 2, 0))
            act.activation(sq0[:, 0:4, :], xT[:, 0:4, :], ACT.Square).then_inc(sq_ready, 1)
            evacuated(act, ("xt", 2, 1))
            act.activation(sq0[:, 4:8, :], xT[:, 4:8, :], ACT.Square).then_inc(sq_ready, 1)

            def norm_act(i, hsrc):
                seen(act, ("norm", i))
                if i == 0:
                    act.wait_ge(con_in, 16)
                ins = act.activation(rstd[:, :], bank(("norm", i))[:, 0:T], ACT.Sqrt, bias=eps)
                free(ins)
                if i < 2:
                    for k in range(2):
                        act.wait_ge(h_ready, 2 * i + k + 1)
                        act.activation(h_hi[:, 4 * k:4 * k + 4, :], hsrc[:, 4 * k:4 * k + 4, :], ACT.Copy).then_inc(hhi_ready, 1)

            hi(0)
            norm_act(0, hf)
            hi(1)

            def pair_slot(i):
                return i % 2

            for w in range(NMIX):
                s, i = UNITS[w]
                hi(w + 2)
                if w > GRET and w <= GRET + 16:
                    f = w - 1 - GRET
                    act.wait_ge(y_ready, f + 1)
                    act.activation(on_hi[:, f, :], oT[:, f, :], ACT.Copy).then_inc(yhi_ready, 1)
                if w > FIRST["cout"] and w <= FIRST["cout"] + 8:
                    f = w - 1 - FIRST["cout"]
                    act.wait_ge(m_ready, f + 1)
                    act.activation(m_hi[:, f, :], yb[:, f, :], ACT.Copy).then_inc(mhi_ready, 1)
                if s in ("q", "k"):
                    p = (0 if s == "q" else 4) + i // 2
                    if i % 2 == 0 and p >= 2:
                        act.wait_ge(rot_ready, p - 1)
                    seen(act, ("m", w))
                    free(act.activation(qk[:, p % 2, i % 2, :], bank(("m", w))[:, 0:T], ACT.Copy,
                                        scale=1.0 if s == "q" else DK ** -0.5))
                if s == "v":
                    if i >= 2:
                        seen(act, ("vt", i - 2))
                    seen(act, ("m", w))
                    free(act.activation(vT[:, i % 2, :], bank(("m", w))[:, 0:T], ACT.Copy))
                if s == "glu_b":
                    if i >= 2:
                        evacuated(act, ("m", w - 2 if i % 2 == 0 else w - 2))
                    seen(act, ("m", w))
                    free(act.activation(sg[:, i % 2, :], bank(("m", w))[:, 0:T], ACT.Sigmoid))
                if s == "gret":
                    g = i
                    if g >= 2:
                        evacuated(act, ("m", w - 2))
                    seen(act, ("m", w))
                    act.activation(sg[:, g % 2, :], bank(("m", w))[:, 0:T], ACT.Sigmoid).then_inc(sig_ready, 1)
                if s == "ret" and i % 2 == 1:
                    seen(act, ("m", w))
                    if i == 1:
                        act.wait_ge(ylo_ready, ET)
                    free(act.activation(yb[:, i // 2, :], bank(("m", w))[:, 0:T], ACT.Copy))
                if s == "gate_b":
                    if i >= 2:
                        evacuated(act, ("m", w - 2))
                    seen(act, ("m", w))
                    act.activation(sg[:, i % 2, :], bank(("m", w))[:, 0:T], ACT.Sigmoid,
                                   bias=par[:, PAR["b_gates"] + 8 + i:PAR["b_gates"] + 9 + i]).then_inc(sig_ready, 1)
                if s == "gate_a":
                    seen(act, ("m", w))
                    free(act.activation(ga[:, i, :], bank(("m", w))[:, 0:T], ACT.Sigmoid,
                                        bias=par[:, PAR["b_gates"] + i:PAR["b_gates"] + 1 + i]))
                if 2 <= w < 6:
                    r, hf2 = (w - 2) // 2, w % 2
                    seen(act, ("sc", r, hf2))
                    free(act.activation(stT[:, 4 * hf2:4 * hf2 + 4, r * 120:(r + 1) * 120],
                                        bank(("sc", r, hf2))[:, 0:480].rearrange("p (f n) -> p f n", f=4), ACT.Copy))
                if GLU <= w < EXTRA_END:
                    k = w - GLU
                    if k < NH:
                        for tt in range(3):
                            nt = min(128, TP - TOKENS[tt][0])
                            nm = ("kt", k, 0 if tt < 2 else 1)
                            if tt == 0 and k >= 2:
                                seen(act, ("S", k - 2, 1))
                            seen(act, nm)
                            col = tt * DK if tt < 2 else 0
                            ins = act.activation(k_tok[0:nt, k % 2, tt, :], bank(nm)[0:nt, col:col + DK], ACT.Copy,
                                                 scale=kdecay[0:nt, tt, k:k + 1])
                            if tt:
                                free(ins)
                    if 1 <= k <= NH:
                        h = k - 1
                        for et in range(4):
                            seen(act, ("o", h, et))
                            free(act.activation(oT[:, 4 * h + et, 0:TP], bank(("o", h, et))[:, 0:TP], ACT.Copy))
                        for dt in range(2):
                            seen(act, ("S", h, dt))
                            if h >= 1:
                                act.wait_ge(Sp_stored[dt], 16 * h)
                            free(act.activation(S_out[:, dt, :], bank(("S", h, dt))[:, :], ACT.Copy))
                    if k >= 4 and k % 4 == 0 and k <= 16:
                        h = k // 4 - 1
                        act.wait_ge(S_used, 4 * h + 4)
                        if h >= 1:
                            seen(act, ("ot", h - 1))
                        act.activation(osb[:, :], o_samp[0:NSAMP, :], ACT.Copy).then_inc(osb_ready, 1)
                    if k >= 5 and (k - 5) % 4 == 0 and k <= 17:
                        h = (k - 5) // 4
                        seen(act, ("ot", h))
                        free(act.activation(oT[:, 4 * h:4 * h + 4, TP:T],
                                            bank(("ot", h))[:, 0:32].rearrange("p (f n) -> p f n", f=4), ACT.Copy))
                    if k >= 6 and (k - 6) % 4 == 0 and k <= 18:
                        h = (k - 6) // 4
                        evacuated(act, ("gm", h))
                        if h >= 1:
                            seen(act, ("gv", h - 1))
                        act.activation(gsq[:, :, :], oT[:, 4 * h:4 * h + 4, :], ACT.Square).then_inc(osq_ready, 1)
                    if k >= 7 and (k - 7) % 4 == 0 and k <= 19:
                        h = (k - 7) // 4
                        seen(act, ("gv", h))
                        if h >= 1:
                            act.wait_ge(std_ready, h)
                        free(act.activation(gstd[:, :], bank(("gv", h))[:, 0:T], ACT.Sqrt, bias=eps))
                    if k in (20, 21):
                        q = k - 20
                        if q == 0:
                            act.wait_ge(Sp_stored[0], 16 * NH)
                            act.wait_ge(Sp_stored[1], 16 * NH)
                        seen(act, ("ut", q))
                        free(act.activation(utok[0:PAD + NSAMP, q, :], bank(("ut", q))[0:PAD + NSAMP, :], ACT.Copy))
                if GLU - 1 <= w < GRET - 1:
                    s2 = w - GLU + 1
                    act.wait_ge(S_in[s2 % 2], 32 * (s2 // 2 + 1))
                    v = S_ring[:, s2 % 2].rearrange("p b t e -> p (b t e)")
                    act.activation(v, v, ACT.Copy, scale=GAMMA[s2 // 4]).then_inc(S_scaled, 1)
                if w == FIRST["cout"] - 4:
                    evacuated(act, ("lm",))
                    for j in range(2):
                        act.wait_ge(S_stored[j], 16 * 16)
                    act.activation(ln_sq[:, :, :], conv[:, :, :], ACT.Square).then_inc(csq_ready, 1)
                if w == FIRST["cout"] - 3:
                    seen(act, ("lv",))
                    free(act.activation(rstd[:, :], bank(("lv",))[:, 0:T], ACT.Sqrt, bias=eps))
                if w == FIRST["cout"] - 2:
                    act.wait_ge(cz_ready, 1)
                    for f in range(KT):
                        g = par[:, PAR["ln_g"] + f:PAR["ln_g"] + f + 1]
                        b = par[:, PAR["ln_b"] + f:PAR["ln_b"] + f + 1]
                        act.activation(ln_sq[:, f, :], conv[:, f, :], ACT.Sigmoid, scale=g, bias=b).then_inc(csig_ready, 1)
                if w == FIRST["cout"] - 1:
                    for f in range(KT):
                        act.wait_ge(cz_ready, 2 + f)
                        act.activation(c_hi[:, f, :], conv[:, f, :], ACT.Copy).then_inc(chi_ready, 1)

            for k in range(2):
                evacuated(act, ("m", FIRST["wo"] + 4 * k + 3))
                act.activation(sq1[:, 4 * k:4 * k + 4, :], xT[:, 4 * k:4 * k + 4, :], ACT.Square).then_inc(sq_ready, 1)
            norm_act(1, h2f)
            hi(NMIX + 2)
            seen(act, ("logit",))
            act.wait_ge(wr_in, 64)
            free(act.activation(lgT[:, :], bank(("logit",))[0:20, 0:T], ACT.Identity, bias=br[:, 0:1]))
            act.wait_ge(ex_ready, 1)
            act.activation(rt[:, :, 0:4], rt[:, :, 0:4], ACT.Exp).then_inc(ex_ready, 1)
            act.wait_ge(d_ready, 1)
            act.activation(rt[:, :, 8:9], rt[:, :, 8:9], ACT.Exp).then_inc(d_ready, 1)
            for e in range(NE):
                seen(act, ("cb", e))
                free(act.activation(comb_b[:, e, :], bank(("cb", e))[:, 0:T], ACT.Copy))

            pend = []
            for w in range(NMIX, len(UNITS)):
                s, e, i = UNITS[w]
                if w > NMIX:
                    hi(w + 2)
                g = 4 * e + i
                if s == "g":
                    if g >= 2:
                        evacuated(act, g_tile(g - 2))
                    seen(act, ("m", w))
                    act.activation(sg[:, g % 2, :], bank(("m", w))[:, 0:T], ACT.Sigmoid).then_inc(sig_ready, 1)
                if s == "u":
                    evacuated(act, ("m", w))
                    if g >= 8:
                        unit_used(act, NMIX + 12 * (e - 2) + 11)
                    act.activation(a_hi[:, e % 2, i, :], a_f[:, g % 2, :], ACT.Copy).then_inc(ahi_ready, 1)
            for k in range(2):
                evacuated(act, ("m", len(UNITS) - 3 + 2 * k, 1))
                act.activation(sq1[:, 4 * k:4 * k + 4, :], xT[:, 4 * k:4 * k + 4, :], ACT.Square).then_inc(sq_ready, 1)
            norm_act(2, None)
            for tt, (t0, nt) in enumerate(TOKENS):
                seen(act, ("yt", tt, 0))
                free(act.activation(y_tok[0:nt, tt, 0:512], bank(("yt", tt, 0))[0:nt, :], ACT.Copy))

        @block.vector
        def _(dve):
            n = {"chain": 0, "conv": 0, "lo": 0}

            def link(ins):
                n["chain"] += 1
                ins.then_inc(dve_chain, 1)
                dve.wait_ge(dve_chain, n["chain"])

            def free(ins):
                ins.then_inc(dve_freed, 1)

            def lo(w):
                if w >= len(UNITS):
                    return
                dve.wait_ge(hi_ready, w + 1)
                dve.tensor_tensor(part_view(w_lo, w), raw_view(w), part_view(w_hi, w).bitcast(f32), ALU.subtract).then_inc(lo_ready, 1)

            convs = []
            for p in range(4):
                for t in range(CW):
                    convs += [(2 * p, t), (2 * p + 1, t)]

            def conv_steps(k):
                for _ in range(k):
                    c = n["conv"]
                    if c >= len(convs):
                        return
                    f, t = convs[c]
                    n["conv"] += 1
                    w_t = cw[:, f, t:t + 1]
                    out, src = conv[:, f, 0:TP], u[:, f, t:t + TP]
                    if t == 0:
                        dve.tensor_scalar(out, src, w_t, par[:, PAR["conv_b"] + f:PAR["conv_b"] + f + 1],
                                          ALU.mult, ALU.add).then_inc(conv_step, 1)
                    else:
                        dve.wait_ge(conv_step, c - 1)
                        dve.scalar_tensor_tensor(out=out, in0=src, scalar=w_t, in1=out, op0=ALU.mult,
                                                 op1=ALU.add).then_inc(conv_step, 1)

            dve.memset(u[:, :, 0:PAD], 0.0)
            dve.memset(lg[:, :, :], 0.0) if False else None
            seen(dve, ("par",))
            free(dve.tensor_copy(par[:, :], bank(("par",))[:, 0:NPAR]))
            for tt, (t0, nt) in enumerate(TOKENS):
                seen(dve, ("xt", tt, 1))
                src = bank(("xt", tt, 1))[:, :].rearrange("p (f n) -> p f n", f=4)[:, :, 0:nt]
                free(dve.tensor_copy(xT[:, 4:8, t0:t0 + nt], src))

            def norm_dve(i, name, dst):
                evacuated(dve, ("norm", i))
                link(dve.reciprocal(rstd[:, :], rstd[:, :]))
                for f in range(KT):
                    g = par[:, PAR[name] + f:PAR[name] + f + 1]
                    ins = dve.scalar_tensor_tensor(out=dst[:, f, :], in0=xT[:, f, :], scalar=g, in1=rstd[:, :],
                                                   op0=ALU.mult, op1=ALU.mult)
                    if f % 4 == 3:
                        ins.then_inc(h_ready, 1)
                if i < 2:
                    for k in range(2):
                        dve.wait_ge(hhi_ready, 2 * i + k + 1)
                        sl = slice(4 * k, 4 * k + 4)
                        dve.tensor_tensor(h_lo[:, sl, :], dst[:, sl, :], h_hi[:, sl, :].bitcast(f32), ALU.subtract).then_inc(hlo_ready, 1)

            lo(0)
            evacuated(dve, ("par",))
            norm_dve(0, "norm_mix", hf)
            lo(1)
            cos2 = cst("cos").rearrange("p (a t) -> p a t", a=1).broadcast_to([128, 2, T])
            sin2 = cst("sin").rearrange("p (a t) -> p a t", a=1).broadcast_to([128, 2, T])

            for w in range(NMIX):
                s, i = UNITS[w]
                lo(w + 2)
                if w > GRET and w <= GRET + 16:
                    f = w - 1 - GRET
                    dve.wait_ge(yhi_ready, f + 1)
                    dve.tensor_tensor(on_lo[:, f, :], oT[:, f, :], on_hi[:, f, :].bitcast(f32), ALU.subtract).then_inc(ylo_ready, 1)
                if w > FIRST["cout"] and w <= FIRST["cout"] + 8:
                    f = w - 1 - FIRST["cout"]
                    dve.wait_ge(mhi_ready, f + 1)
                    dve.tensor_tensor(m_lo[:, f, :], yb[:, f, :], m_hi[:, f, :].bitcast(f32), ALU.subtract).then_inc(mlo_ready, 1)
                if s in ("q", "k") and i % 2 == 1:
                    p = (0 if s == "q" else 4) + i // 2
                    dst = qT if s == "q" else kT
                    evacuated(dve, ("m", w))
                    if p >= 1:
                        dve.wait_ge(rot_ready, p)
                    dve.tensor_tensor(rot[:, 0, :, :], qk[:, p % 2, :, :], cos2, ALU.mult)
                    link(dve.tensor_tensor(rot[:, 1, :, :], qk[:, p % 2, :, :], sin2, ALU.mult))
                    dve.tensor_tensor(dst[:, i - 1, :], rot[:, 0, 0, :], rot[:, 1, 1, :], ALU.subtract)
                    dve.tensor_tensor(dst[:, i, :], rot[:, 1, 0, :], rot[:, 0, 1, :], ALU.add).then_inc(rot_ready, 1)
                if s == "glu_a":
                    evacuated(dve, ("m", w - 2))
                    seen(dve, ("m", w))
                    free(dve.tensor_tensor(u[:, i, PAD:UW], bank(("m", w))[:, 0:T], sg[:, i % 2, :], ALU.mult))
                if s == "gret":
                    seen(dve, ("m", w))
                    dve.wait_ge(sig_ready, i + 1)
                    if i >= 1:
                        dve.wait_ge(y_ready, i)
                    ins = dve.tensor_tensor(tg[:, i % 2, :], bank(("m", w))[:, 0:T], sg[:, i % 2, :], ALU.mult)
                    free(ins)
                    evacuated(dve, ("m", w))
                    g = par[:, PAR["gn_g"] + i:PAR["gn_g"] + i + 1]
                    dve.scalar_tensor_tensor(out=oT[:, i, :], in0=oT[:, i, :], scalar=g, in1=tg[:, i % 2, :],
                                             op0=ALU.mult, op1=ALU.mult).then_inc(y_ready, 1)
                if s == "gate_b":
                    evacuated(dve, ("m", FIRST["ret"] + 2 * i + 1))
                    dve.wait_ge(sig_ready, 16 + i + 1)
                    free(dve.tensor_tensor(yb[:, i, :], yb[:, i, :], sg[:, i % 2, :], ALU.mult))
                if s == "cout":
                    seen(dve, ("m", w))
                    evacuated(dve, ("m", FIRST["gate_a"] + i))
                    free(dve.tensor_tensor(ga[:, i, :], bank(("m", w))[:, 0:T], ga[:, i, :], ALU.mult))
                    evacuated(dve, ("m", w))
                    dve.tensor_tensor(yb[:, i, :], yb[:, i, :], ga[:, i, :], ALU.add).then_inc(m_ready, 1)
                if s == "wo":
                    seen(dve, ("m", w))
                    ins = dve.tensor_tensor(xT[:, i, :], bank(("m", w))[:, 0:T], xT[:, i, :], ALU.add)
                    free(ins)
                if w == 1:
                    seen(dve, ("cw",))
                    free(dve.tensor_copy(cw[:, :, :], bank(("cw",))[:, 0:KT * CW].rearrange("p (f t) -> p f t", f=KT)))
                if w in (6, 7):
                    if w == 6:
                        evacuated(dve, ("sc", 1, 1))
                        evacuated(dve, ("cw",))
                    for f in range(4 * (w - 6), 4 * (w - 6) + 4):
                        wb = cw[:, f:f + 1, 0:CW - 1].broadcast_to([128, NSAMP, CW - 1])
                        v = stT[:, f, :].rearrange("p (b t) -> p b t", b=NSAMP)
                        last = dve.tensor_tensor(v, v, wb, ALU.mult)
                    link(last)
                    sl = slice(4 * (w - 6), 4 * (w - 6) + 4)
                    link(dve.tensor_reduce(out=csamp[:, sl, :], in_=stT[:, sl, :].rearrange("p f (b t) -> p f b t", b=NSAMP),
                                      axis=AX.X, op=ALU.add))
                    for f in range(4 * (w - 6), 4 * (w - 6) + 4):
                        last = dve.tensor_scalar(csamp[:, f, :], csamp[:, f, :], par[:, PAR["conv_b"] + f:PAR["conv_b"] + f + 1],
                                                 None, ALU.add)
                    link(last)
                if FIRST["v"] < w <= FIRST["v"] + 16:
                    j = w - 1 - FIRST["v"]
                    seen(dve, ("vt", j))
                    b = bank(("vt", j))
                    dve.tensor_copy(v_tok[:, 0:2, j * 128:(j + 1) * 128], b[:, 0:256].rearrange("p (t n) -> p t n", t=2))
                    free(dve.tensor_copy(v_tok[0:24, 2, j * 128:(j + 1) * 128], b[0:24, 256:384]))
                if w == FIRST["v"]:
                    dve.wait_ge(rot_ready, 8)
                    for b in range(NSAMP):
                        dst = qm[:, :, b, :]
                        idb = ident[:, 0:1].broadcast_to([128, 1]) if False else None
                    dve.memset(qm[:, :, :, :], 0.0)
                    link(dve.memset(rstd[:, 0:1], 0.0))
                    for b in range(NSAMP):
                        last = dve.tensor_copy(qm[:, :, b, b:b + 1], qT[:, :, TP + b:TP + b + 1])
                    last.then_inc(qm_ready, 1)
                if GLU <= w < EXTRA_END:
                    k = w - GLU
                    if k < NH:
                        if k >= 1:
                            seen(dve, ("o", k - 1, 3))
                        seen(dve, ("score", k))
                        b = bank(("score", k))
                        dve.tensor_tensor(P[:, 0:272], b[:, 0:272], mask[:, k, 0:272], ALU.mult)
                        dve.tensor_tensor(P[:, 272:416], b[:, 272:416], mask[:, k, 0:144], ALU.mult)
                        free(dve.tensor_tensor(P[0:16, 416:432], b[0:16, 416:432], mask[0:16, k, 0:16], ALU.mult))
                    if k < 16:
                        h = k // 4
                        dve.wait_ge(S_scaled, k + 1)
                        for j in range(2):
                            smp = 2 * (k % 4) + j
                            seen(dve, ("vb", k, j))
                            for dt in range(2):
                                st = S_ring[:, k % 2, j, dt, :]
                                f = 2 * h + dt
                                ins = dve.scalar_tensor_tensor(out=st, in0=bank(("vb", k, j))[:, :],
                                                               scalar=kT[:, f, TP + smp:TP + smp + 1], in1=st,
                                                               op0=ALU.mult, op1=ALU.add)
                            free(ins)
                    if k >= 6 and (k - 6) % 4 == 0 and k <= 18:
                        h = (k - 6) // 4
                        seen(dve, ("gm", h))
                        evacuated(dve, ("ot", h))
                        mb = bank(("gm", h))[:, 0:T].rearrange("p (a t) -> p a t", a=1).broadcast_to([128, 4, T])
                        v = oT[:, 4 * h:4 * h + 4, :]
                        free(dve.tensor_tensor(v, v, mb, ALU.subtract))
                    if k >= 7 and (k - 7) % 4 == 0 and k <= 19:
                        h = (k - 7) // 4
                        evacuated(dve, ("gv", h))
                        link(dve.reciprocal(rstd[:, :], gstd[:, :]))
                        rb = rstd[:, :].rearrange("p (a t) -> p a t", a=1).broadcast_to([128, 4, T])
                        v = oT[:, 4 * h:4 * h + 4, :]
                        dve.wait_ge(osq_ready, h + 1)
                        dve.tensor_tensor(v, v, rb, ALU.mult).then_inc(std_ready, 1)
                        dve.wait_ge(std_ready, h + 1)
                conv_steps(conv_quota(w))
                if w == FIRST["cout"] - 5:
                    conv_steps(len(convs))
                    for f in range(KT):
                        last = dve.scalar_tensor_tensor(out=conv[:, f, TP:T], in0=u[:, f, PAD + TP:UW], scalar=cw[:, f, CW - 1:CW],
                                                        in1=csamp[:, f, :], op0=ALU.mult, op1=ALU.add)
                    last.then_inc(conv_step, 1)
                if w == FIRST["cout"] - 4:
                    seen(dve, ("lm",))
                    mb = bank(("lm",))[:, 0:T].rearrange("p (a t) -> p a t", a=1).broadcast_to([128, KT, T])
                    free(dve.tensor_tensor(conv[:, :, :], conv[:, :, :], mb, ALU.subtract))
                if w == FIRST["cout"] - 3:
                    evacuated(dve, ("lv",))
                    link(dve.reciprocal(rstd[:, :], rstd[:, :]))
                    rb = rstd[:, :].rearrange("p (a t) -> p a t", a=1).broadcast_to([128, KT, T])
                    dve.wait_ge(csq_ready, 1)
                    dve.tensor_tensor(conv[:, :, :], conv[:, :, :], rb, ALU.mult).then_inc(cz_ready, 1)
                    dve.wait_ge(cz_ready, 1)
                if w == FIRST["cout"] - 1:
                    for f in range(KT):
                        g = par[:, PAR["ln_g"] + f:PAR["ln_g"] + f + 1]
                        b = par[:, PAR["ln_b"] + f:PAR["ln_b"] + f + 1]
                        dve.wait_ge(csig_ready, f + 1)
                        link(dve.tensor_scalar(conv[:, f, :], conv[:, f, :], g, b, ALU.mult, ALU.add))
                        dve.tensor_tensor(conv[:, f, :], conv[:, f, :], ln_sq[:, f, :], ALU.mult).then_inc(cz_ready, 1)
                    for f in range(KT):
                        dve.wait_ge(chi_ready, f + 1)
                        dve.tensor_tensor(c_lo[:, f, :], conv[:, f, :], c_hi[:, f, :].bitcast(f32), ALU.subtract).then_inc(clo_ready, 1)

            norm_dve(1, "norm_ffn", h2f)
            lo(NMIX + 2)
            link(dve.memset(lg[:, :, :], 0.0))
            seen(dve, ("lt",))
            b = bank(("lt",))
            dve.tensor_copy(lg[:, 0:2, :], b[:, 0:40].rearrange("p (t n) -> p t n", t=2))
            free(dve.tensor_copy(lg[0:24, 2, :], b[0:24, 40:60]))
            evacuated(dve, ("lt",))
            rank = cst("rank").rearrange("p (a k) -> p a k", a=1).broadcast_to([128, 3, 4])
            L4, F16 = lg[:, :, 0:4], lg[:, :, 4:20]
            ex, mx4, og, o1, o2, tmp = rt[:, :, 0:4], rt[:, :, 12:13], rt[:, :, 16:20], rt[:, :, 20:24], rt[:, :, 24:28], rt[:, :, 28:32]
            dd, v1, v2, pg, w1, w2, sel = rt[:, :, 8:9], rt[:, :, 9:10], rt[:, :, 10:11], rt[:, :, 11:12], rt[:, :, 13:14], rt[:, :, 14:15], rt[:, :, 32:36]
            prod = rt[:, :, 48:64]

            def bc(x, k=4):
                return x.broadcast_to([128, 3, k])

            def first_max(out, src, top):
                link(dve.tensor_tensor(tmp, src, bc(top), ALU.is_equal))
                link(dve.tensor_tensor(tmp, tmp, rank, ALU.mult))
                link(dve.tensor_reduce(out=w2, in_=tmp, axis=AX.X, op=ALU.max))
                link(dve.tensor_tensor(out, tmp, bc(w2), ALU.is_equal))

            link(dve.tensor_reduce(out=mx4, in_=L4, axis=AX.X, op=ALU.max))
            dve.tensor_tensor(ex, L4, bc(mx4), ALU.subtract).then_inc(ex_ready, 1)
            first_max(og, L4, mx4)
            link(dve.tensor_tensor(prod.rearrange("p t (g i) -> p t g i", g=4), F16.rearrange("p t (g i) -> p t g i", g=4),
                                   og.rearrange("p t (g a) -> p t g a", a=1).broadcast_to([128, 3, 4, 4]), ALU.mult))
            link(dve.tensor_reduce(out=sel, in_=prod.rearrange("p t (g i) -> p t i g", g=4), axis=AX.X, op=ALU.add))
            link(dve.tensor_reduce(out=v1, in_=sel, axis=AX.X, op=ALU.max))
            first_max(o1, sel, v1)
            link(dve.scalar_tensor_tensor(out=sel, in0=o1, scalar=-3.0e38, in1=sel, op0=ALU.mult, op1=ALU.add))
            link(dve.tensor_reduce(out=v2, in_=sel, axis=AX.X, op=ALU.max))
            first_max(o2, sel, v2)
            dve.tensor_tensor(dd, v2, v1, ALU.subtract).then_inc(d_ready, 1)
            dve.wait_ge(ex_ready, 2)
            link(dve.tensor_reduce(out=pg, in_=ex, axis=AX.X, op=ALU.add))
            link(dve.reciprocal(pg, pg))
            dve.wait_ge(d_ready, 2)
            link(dve.tensor_scalar(w1, dd, 1.0, None, ALU.add))
            link(dve.reciprocal(w1, w1))
            link(dve.tensor_tensor(w1, w1, pg, ALU.mult))
            link(dve.tensor_tensor(w2, w1, dd, ALU.mult))
            link(dve.tensor_tensor(o1, o1, bc(w1), ALU.mult))
            link(dve.tensor_tensor(o2, o2, bc(w2), ALU.mult))
            link(dve.tensor_tensor(o1, o1, o2, ALU.add))
            dve.tensor_tensor(comb[:, :, :].rearrange("p t (g i) -> p t g i", g=4),
                              og.rearrange("p t (g a) -> p t g a", a=1).broadcast_to([128, 3, 4, 4]),
                              o1.rearrange("p t (a i) -> p t a i", a=1).broadcast_to([128, 3, 4, 4]), ALU.mult).then_inc(comb_ready, 1)

            def a_low(g):
                e, i = g // 4, g % 4
                dve.wait_ge(ahi_ready, g + 1)
                dve.tensor_tensor(a_lo[:, e % 2, i, :], a_f[:, g % 2, :], a_hi[:, e % 2, i, :].bitcast(f32), ALU.subtract).then_inc(alo_ready, 1)

            yc = 0
            for w in range(NMIX, len(UNITS)):
                s, e, i = UNITS[w]
                if w > NMIX:
                    lo(w + 2)
                g = 4 * e + i
                t = t_f[:, g % 2, :]
                if s == "g":
                    if g >= 2:
                        dve.wait_ge(alo_ready, g - 1)
                    dve.wait_ge(sig_ready, 24 + g + 1)
                    free(dve.tensor_tensor(t, bank(("m", w))[:, 0:T], sg[:, g % 2, :], ALU.mult))
                if s == "u":
                    evacuated(dve, ("cb", e))
                    evacuated(dve, ("m", w - 2))
                    link(dve.tensor_tensor(t, t, comb_b[:, e, :], ALU.mult))
                    seen(dve, ("m", w))
                    free(dve.tensor_tensor(a_f[:, g % 2, :], bank(("m", w))[:, 0:T], t, ALU.mult))
                    a_low(g)
                if s == "d":
                    for j in range(2):
                        seen(dve, ("m", w, j))
                        f = 2 * i + j
                        if e >= 1:
                            dve.wait_ge(dve_freed, TILE[("m", w - 12, j)][2])
                        free(dve.tensor_tensor(xT[:, f, :], bank(("m", w, j))[:, 0:T], xT[:, f, :], ALU.add))
            norm_dve(2, "norm_final", h2f)
            for tt, (t0, nt) in enumerate(TOKENS):
                seen(dve, ("yt", tt, 1))
                free(dve.tensor_copy(y_tok[0:nt, tt, 512:1024], bank(("yt", tt, 1))[0:nt, :]))

        @block.tensor
        def _(pe):
            at = {"i": 0}

            def opened(name):
                i = TILE[name][0]
                assert i == at["i"], (name, TILES[at["i"]])
                at["i"] += 1
                if i >= BANKS:
                    evacuated(pe, TILES[i - BANKS][0])
                return banks[i % BANKS]

            def done(ins):
                ins.then_inc(tile_ready, 1)

            def passes(out, w, ks, x_hi, x_lo, k0=0, m=None, first=True, last=True):
                hi, lo = part_view(w_hi, w), part_view(w_lo, w)
                cols = slice(0, 128) if m is None else slice(m * 128, (m + 1) * 128)
                for k in range(ks):
                    for j, (a, b) in enumerate(((hi, x_hi), (hi, x_lo), (lo, x_hi))):
                        ins = pe.matmul(out, a[:, k, cols], b[:, k0 + k, :], start=first and k == 0 and j == 0,
                                        stop=last and k == ks - 1 and j == 2)
                return ins

            pe.wait_ge(con_in, 16)
            pe.wait_ge(par_in, 128)
            b = opened(("par",))
            done(pe.transpose(b[:, 0:NPAR], par_rows[:, :], ident[0:NPAR, 0:NPAR]))
            pe.wait_ge(x_in, 80)
            for tt, (t0, nt) in enumerate(TOKENS):
                for hf2 in range(2):
                    b = opened(("xt", tt, hf2))
                    for f in range(4):
                        col = (4 * hf2 + f) * 128
                        ins = pe.transpose(b[:, f * 128:f * 128 + nt], x_tok[0:nt, tt, col:col + 128], ident[0:nt, 0:nt])
                    done(ins)

            def norm_pe(i, sq):
                b = opened(("norm", i))
                for f in range(KT):
                    if f % 4 == 0:
                        pe.wait_ge(sq_ready, 2 * i + f // 4 + 1)
                    ins = pe.matmul(b[:, 0:T], cst("mean_d"), sq[:, f, :], start=f == 0, stop=f == KT - 1)
                done(ins)

            norm_pe(0, sq0)

            def samp_o(s):
                h = s // 4
                evacuated(pe, ("vb", s, 1))
                if s % 4 == 0 and h >= 1:
                    pe.wait_ge(osb_ready, h)
                for j in range(2):
                    smp = 2 * (s % 4) + j
                    for dt in range(2):
                        ins = pe.matmul(o_samp[0:NSAMP, :], qm[:, 2 * h + dt, smp, :], S_ring[:, s % 2, j, dt, :],
                                        start=smp == 0 and dt == 0, stop=smp == NSAMP - 1 and dt == 1)
                ins.then_inc(S_used, 1)

            for w in range(NMIX):
                s, i = UNITS[w]
                if w == 0:
                    pe.wait_ge(hlo_ready, 2)
                pe.wait_ge(lo_ready, w + 1)
                if s == "ret":
                    if i == 0:
                        pe.wait_ge(ylo_ready, ET - 1)
                    if i == 1:
                        pe.wait_ge(ylo_ready, ET)
                    if i % 2 == 0:
                        b = opened(("m", w + 1))
                        passes(b[:, 0:T], w, 8, on_hi, on_lo, last=False)
                    else:
                        done(passes(b[:, 0:T], w, 8, on_hi, on_lo, k0=8, first=False))
                else:
                    xh, xl = h_hi, h_lo
                    if s == "cout":
                        xh, xl = c_hi, c_lo
                        if i == 0:
                            pe.wait_ge(clo_ready, KT)
                    if s == "wo":
                        xh, xl = m_hi, m_lo
                        if i == 0:
                            pe.wait_ge(mlo_ready, KT)
                    b = opened(("m", w))
                    done(passes(b[:, 0:T], w, 8, xh, xl))
                if w == 1:
                    pe.wait_ge(cw_in, 16)
                    b = opened(("cw",))
                    for f in range(KT):
                        ins = pe.transpose(b[:, f * CW:(f + 1) * CW], cw_rows[:, f * 128:(f + 1) * 128], ident[0:CW, 0:CW])
                    done(ins)
                if 2 <= w < 6:
                    r, hf2 = (w - 2) // 2, w % 2
                    pe.wait_ge(sc_in, 32)
                    b = opened(("sc", r, hf2))
                    for f in range(4):
                        col = (4 * hf2 + f) * 128
                        ins = pe.transpose(b[:, f * 120:(f + 1) * 120], sc_rows[:, r, col:col + 128], ident[0:120, 0:120])
                    done(ins)
                if FIRST["v"] < w <= FIRST["v"] + 16:
                    j = w - 1 - FIRST["v"]
                    evacuated(pe, ("m", w - 1))
                    b = opened(("vt", j))
                    for tt, (t0, nt) in enumerate(TOKENS):
                        ins = pe.transpose(b[0:nt, tt * 128:tt * 128 + 128], vT[:, j % 2, t0:t0 + nt], ident)
                    done(ins)
                if GLU <= w < EXTRA_END:
                    k = w - GLU
                    if k < NH:
                        h = k
                        pe.wait_ge(rot_ready, 8)
                        b = opened(("score", h))
                        col = 0
                        for t0, nt in ((0, 128), (128, 128), (256, 16)):
                            for dt in range(2):
                                ins = pe.matmul(b[0:nt, col:col + TP - t0], kT[:, 2 * h + dt, t0:t0 + nt],
                                                qT[:, 2 * h + dt, t0:TP], start=dt == 0, stop=dt == 1)
                            col += TP - t0
                        done(ins)
                        b = opened(("kt", h, 0))
                        for tt in range(2):
                            for dt in range(2):
                                c0 = tt * DK + dt * 128
                                ins = pe.transpose(b[:, c0:c0 + 128], kT[:, 2 * h + dt, tt * 128:(tt + 1) * 128], ident)
                        done(ins)
                        b = opened(("kt", h, 1))
                        for dt in range(2):
                            ins = pe.transpose(b[0:16, dt * 128:dt * 128 + 128], kT[:, 2 * h + dt, 256:272], ident)
                        done(ins)
                    if 1 <= k <= NH:
                        h = k - 1
                        evacuated(pe, ("vt", 15))
                        evacuated(pe, ("score", h))
                        for et in range(4):
                            b = opened(("o", h, et))
                            col = 0
                            for tt, (t0, nt) in enumerate(((0, 128), (128, 128), (256, 16))):
                                e0 = h * DV + et * 128
                                ins = pe.matmul(b[:, t0:TP], v_tok[0:nt, tt, e0:e0 + 128], P[0:nt, col:col + TP - t0],
                                                start=tt == 0, stop=tt == 2)
                                col += TP - t0
                            done(ins)
                        evacuated(pe, ("kt", h, 1))
                        for dt in range(2):
                            b = opened(("S", h, dt))
                            for tt, nt in enumerate((128, 128, 16)):
                                ins = pe.matmul(b[:, :], k_tok[0:nt, h % 2, tt, dt * 128:(dt + 1) * 128],
                                                v_tok[0:nt, tt, h * DV:(h + 1) * DV], start=tt == 0, stop=tt == 2)
                            done(ins)
                    if k == 0:
                        pe.wait_ge(qm_ready, 1)
                        evacuated(pe, ("vt", 15))
                    if k < 16:
                        h = k // 4
                        for j in range(2):
                            smp = 2 * (k % 4) + j
                            b = opened(("vb", k, j))
                            done(pe.matmul(b[:, :], ident[0:24, 16 + smp:17 + smp].broadcast_to([24, 128]),
                                           v_tok[0:24, 2, h * DV:(h + 1) * DV], start=True, stop=True))
                    if 1 <= k <= 16:
                        samp_o(k - 1)
                    if k >= 5 and (k - 5) % 4 == 0 and k <= 17:
                        h = (k - 5) // 4
                        pe.wait_ge(osb_ready, h + 1)
                        b = opened(("ot", h))
                        for et in range(4):
                            ins = pe.transpose(b[:, et * 8:et * 8 + 8], osb[:, et * 128:(et + 1) * 128], ident[0:8, 0:8])
                        done(ins)
                    if k >= 6 and (k - 6) % 4 == 0 and k <= 18:
                        h = (k - 6) // 4
                        evacuated(pe, ("ot", h))
                        b = opened(("gm", h))
                        for et in range(4):
                            ins = pe.matmul(b[:, 0:T], cst("mean_v"), oT[:, 4 * h + et, :], start=et == 0, stop=et == 3)
                        done(ins)
                    if k >= 7 and (k - 7) % 4 == 0 and k <= 19:
                        h = (k - 7) // 4
                        pe.wait_ge(osq_ready, h + 1)
                        b = opened(("gv", h))
                        for et in range(4):
                            ins = pe.matmul(b[:, 0:T], cst("mean_v"), gsq[:, et, :], start=et == 0, stop=et == 3)
                        done(ins)
                    if k in (20, 21):
                        q = k - 20
                        evacuated(pe, ("m", GRET - 1))
                        b = opened(("ut", q))
                        for f in range(4):
                            ins = pe.transpose(b[0:PAD + NSAMP, f * 128:(f + 1) * 128], u[:, 4 * q + f, TP:UW], ident)
                        done(ins)
                if w == FIRST["cout"] - 4:
                    pe.wait_ge(conv_step, KT * CW + 1)
                    b = opened(("lm",))
                    for f in range(KT):
                        ins = pe.matmul(b[:, 0:T], cst("mean_d"), conv[:, f, :], start=f == 0, stop=f == KT - 1)
                    done(ins)
                if w == FIRST["cout"] - 3:
                    pe.wait_ge(csq_ready, 1)
                    b = opened(("lv",))
                    for f in range(KT):
                        ins = pe.matmul(b[:, 0:T], cst("mean_d"), ln_sq[:, f, :], start=f == 0, stop=f == KT - 1)
                    done(ins)

            norm_pe(1, sq1)
            pe.wait_ge(wr_in, 64)
            pe.wait_ge(h_ready, 4)
            b = opened(("logit",))
            for f in range(KT):
                ins = pe.matmul(b[0:20, 0:T], wr[:, f, :], h2f[:, f, :], start=f == 0, stop=f == KT - 1)
            done(ins)
            evacuated(pe, ("logit",))
            b = opened(("lt",))
            for tt, (t0, nt) in enumerate(TOKENS):
                ins = pe.transpose(b[0:nt, tt * 20:tt * 20 + 20], lgT[:, t0:t0 + nt], ident[0:20, 0:20])
            done(ins)
            pe.wait_ge(comb_ready, 1)
            for e in range(NE):
                b = opened(("cb", e))
                for tt, (t0, nt) in enumerate(TOKENS):
                    ins = pe.matmul(b[:, t0:t0 + nt], comb[0:nt, tt, e:e + 1].broadcast_to([nt, 128]), ident[0:nt, 0:nt],
                                    start=True, stop=True)
                done(ins)
            pe.wait_ge(hlo_ready, 4)
            for w in range(NMIX, len(UNITS)):
                s, e, i = UNITS[w]
                pe.wait_ge(lo_ready, w + 1)
                if s != "d":
                    b = opened(("m", w))
                    done(passes(b[:, 0:T], w, 8, h_hi, h_lo))
                else:
                    pe.wait_ge(alo_ready, 4 * e + 4)
                    for j in range(2):
                        b = opened(("m", w, j))
                        done(passes(b[:, 0:T], w, 4, a_hi[:, e % 2], a_lo[:, e % 2], m=j))
            norm_pe(2, sq1)
            pe.wait_ge(h_ready, 6)
            for tt, (t0, nt) in enumerate(TOKENS):
                for hf2 in range(2):
                    b = opened(("yt", tt, hf2))
                    for f in range(4):
                        ins = pe.transpose(b[0:nt, f * 128:(f + 1) * 128], h2f[:, 4 * hf2 + f, t0:t0 + nt], ident)
                    done(ins)


def g_tile(g):
    e, i = g // 4, g % 4
    return ("m", NMIX + 12 * e + 4 * (i // 2) + i % 2)


_INS = ["x_prompt", "x_sample", "state_ret", "state_conv", "meta_tokens", "norm_mix_g", "w_in", "b_gates", "conv_w",
        "conv_b", "conv_ln_g", "conv_ln_b", "w_conv_out", "ret_gn_g", "w_ret_out", "w_o", "norm_ffn_g", "w_coarse",
        "b_coarse", "w_fine", "b_fine", "w_gate_e", "w_up_e", "w_down_e", "norm_final_g"]
_OUTS = [("y_prompt", (1, SEQ, D)), ("y_sample", (NSAMP, 1, D)), ("ret_prompt", (1, 1, NH, DK, DV)),
         ("conv_prompt", (1, 1, PAD, D)), ("ret_sample", (1, NSAMP, NH, DK, DV)), ("conv_sample", (1, NSAMP, PAD, D))]


def kernel(**inputs):
    import numpy as _np
    import concourse.bacc as _bacc
    from concourse import mybir as _mybir
    from concourse.bass_utils import run_bass_kernel_spmd as _run

    nc = _bacc.Bacc("TRN2", target_bir_lowering=False, num_devices=1)
    arrays, A, O = {}, {}, {}
    for name in _INS:
        a = _np.ascontiguousarray(inputs[name])
        arrays[f"in_{name}"] = a
        A[name] = nc.dram_tensor(f"in_{name}", a.shape, _mybir.dt.from_np(a.dtype), kind="ExternalInput").ap()
    c = constants()
    arrays["constants"] = c
    C = nc.dram_tensor("constants", c.shape, _mybir.dt.from_np(c.dtype), kind="ExternalInput").ap()
    for name, shape in _OUTS:
        O[name] = nc.dram_tensor(f"out_{name}", shape, _mybir.dt.float32, kind="ExternalOutput").ap()
    build(nc, A, C, O)
    r = _run(nc, [arrays], core_ids=[0])
    return tuple(r.results[0][f"out_{name}"] for name, _ in _OUTS)
```

```python
import concourse.bass as bass
from concourse import mybir
from contextlib import ExitStack
import numpy as np

D = 1024
KT = D // 128
SEQ, NMETA, NSAMP = 256, 16, 8
TP = NMETA + SEQ
T = TP + NSAMP
TOKENS = [(0, 128), (128, 128), (256, T - 256)]
NH, DK, DV = 4, 256, 512
ET = NH * DV // 128
CW = 31
PAD = CW - 1
UW = PAD + T
NE, NG, DE = 16, 4, 512
PAST = 2048
EPS = 1e-6
GAMMA = [1.0 - 2.0 ** (-5 - h) for h in range(NH)]
CAP = 128
ROUNDS = -(-T // CAP)
YS = 4
BANKS = 7
WS = 3
ES = 4
LOOK = 3

PAR = {}
_n = 0
for _name, _k in (("norm_mix", 8), ("b_gates", 16), ("conv_b", 8), ("ln_g", 8), ("ln_b", 8), ("gn_g", 16),
                  ("norm_ffn", 8), ("norm_final", 8)):
    PAR[_name] = _n
    _n += _k
NPAR = _n

CON = {}
_n = 0
for _name, _k in (("ident", 128), ("cos", T), ("sin", T), ("mask", NH * TP), ("kdecay", 3 * NH), ("mean_d", 128),
                  ("mean_v", 128), ("eps", 1), ("rank", 4), ("quads", NSAMP)):
    CON[_name] = (_n, _k)
    _n += _k
NCON = _n


MCON = {"before": 0, "ones": 128, "iota": 256}
NMCON = 384


def moe_constants():
    c = np.ones((128, NMCON), np.float32)
    i = np.arange(128)
    c[:, 0:128] = i[:, None] < i[None, :]
    c[:, 256:384] = i[None, :]
    return c


def constants():
    c = np.zeros((128, NCON), np.float32)

    def put(name, a):
        at, k = CON[name]
        c[:, at:at + k] = a

    half = DK // 2
    pos = np.concatenate([np.arange(TP), np.full(NSAMP, PAST)]).astype(np.float32)
    freq = np.power(np.float32(10000.0), -np.arange(half, dtype=np.float32) / np.float32(half)).astype(np.float32)
    ang = (freq[:, None] * pos[None, :]).astype(np.float32).astype(np.float64)
    put("ident", np.eye(128))
    put("cos", np.cos(ang))
    put("sin", np.sin(ang))
    i, j = np.arange(TP)[None, :], np.arange(128)[:, None]
    put("mask", np.concatenate([np.where(i >= j, g ** np.maximum(i - j, 0), 0.0) for g in map(float, GAMMA)], 1))
    kd = np.zeros((128, 3, NH))
    for tt, (t0, n) in enumerate(TOKENS):
        for p in range(min(n, TP - t0)):
            kd[p, tt] = [g ** (TP - 1 - t0 - p) for g in GAMMA]
    put("kdecay", kd.reshape(128, 3 * NH))
    put("mean_d", np.full((128, 128), 1.0 / D))
    put("mean_v", np.full((128, 128), 1.0 / DV))
    put("eps", np.full((128, 1), EPS))
    put("quads", (np.arange(128)[:, None] % 32 == np.arange(NSAMP)[None, :]))
    put("rank", np.tile(np.arange(4, 0, -1), (128, 1)))
    return c


UNITS = []
for _s, _c in (("q", 8), ("k", 8), ("v", 16)):
    UNITS += [(_s, i) for i in range(_c)]
for _j in range(4):
    UNITS += [("glu_b", 2 * _j), ("glu_b", 2 * _j + 1), ("glu_a", 2 * _j), ("glu_a", 2 * _j + 1)]
UNITS += [("gret", i) for i in range(16)] + [("ret", i) for i in range(16)]
UNITS += [("gate_b", i) for i in range(8)] + [("gate_a", i) for i in range(8)]
UNITS += [("cout", i) for i in range(8)] + [("wo", i) for i in range(8)]
NMIX = len(UNITS)
for _r in range(ROUNDS):
    for _e in range(NE + 1):
        if _e < NE:
            UNITS += [("g", _e, _i, _r) for _i in range(4)] + [("u", _e, _i, _r) for _i in range(4)]
        if _e > 0:
            UNITS += [("d", _e - 1, _i, _r) for _i in range(4)]
PER_ROUND = 12 * NE
UNIT = {_u: _w for _w, _u in enumerate(UNITS)}
FIRST = {}
for _w, _u in enumerate(UNITS):
    FIRST.setdefault(_u[0], _w)
GLU, GRET = FIRST["glu_b"], FIRST["gret"]
EXTRA_END = GRET + 16

TILES = []
UNIT_TILE = {}


def _tiles():
    add = TILES.append
    for tt in range(3):
        for hf in range(2):
            add((("xt", tt, hf), "D" if hf else "A"))
    add((("par",), "D"))
    add((("norm", 0), "A"))
    for w in range(NMIX):
        u = UNITS[w]
        s, i = u
        if s == "ret":
            if i % 2:
                add((("m", w), "A"))
        elif s in ("q", "k", "v", "glu_b"):
            add((("m", w), "A"))
        elif s == "gate_b" or s == "glu_a" or s in ("gret", "cout", "wo"):
            add((("m", w), "D"))
        elif s == "gate_a":
            add((("m", w), "A"))
        if w == 1:
            add((("cw",), "D"))
        if 2 <= w < 6:
            add((("sc", (w - 2) // 2, w % 2), "A"))
        if FIRST["v"] < w <= FIRST["v"] + 16:
            add((("vt", w - 1 - FIRST["v"]), "D"))
        if GLU <= w < EXTRA_END:
            k = w - GLU
            if k < NH:
                add((("score", k), "D"))
                add((("kt", k, 0), "A"))
                add((("kt", k, 1), "A"))
            if 1 <= k <= NH:
                for et in range(4):
                    add((("o", k - 1, et), "A"))
                for dt in range(2):
                    add((("S", k - 1, dt), "A"))
            if k < 16:
                add((("vb", k, 0), "D"))
                add((("vb", k, 1), "D"))
            if k >= 5 and (k - 5) % 4 == 0 and k <= 17:
                add((("ot", (k - 5) // 4), "A"))
            if k >= 6 and (k - 6) % 4 == 0 and k <= 18:
                add((("gm", (k - 6) // 4), "D"))
            if k >= 7 and (k - 7) % 4 == 0 and k <= 19:
                add((("gv", (k - 7) // 4), "A"))
            if k in (20, 21):
                add((("ut", k - 20), "A"))
        if w == FIRST["cout"] - 4:
            add((("lm",), "D"))
        if w == FIRST["cout"] - 3:
            add((("lv",), "A"))
    add((("norm", 1), "A"))
    add((("logit",), "A"))
    for tt in range(3):
        for hf in range(2):
            add((("ht", tt, hf), "D"))
    add((("lt",), "D"))
    add((("pos",), "D"))
    for r in range(ROUNDS):
        for j in range(8):
            add((("x", 0, j, r), "A"))
        for e in range(NE + 1):
            if e < NE:
                add((("hg", e, r), "D"))
            if e > 0:
                add((("tr", e - 1, r), "D"))
            if e < NE:
                add((("st", e, r), "A"))
                if e // 2 + 1 < NE // 2:
                    for j in range(4):
                        add((("x", e // 2 + 1, 4 * (e % 2) + j, r), "A"))
            if e % YS == 1 and e > YS:
                for f in range(KT):
                    add((("y", e // YS - 1, f, r), "D"))
            if e < NE:
                add((("hu", e, r), "D"))
            if e > 0:
                for j in range(2):
                    add((("dn", e - 1, j, r), "D"))
        for f in range(KT):
            add((("y", NE // YS - 1, f, r), "D"))


_tiles()
TILE = {}
_cnt = {"A": 0, "D": 0}
for _i, (_name, _f) in enumerate(TILES):
    _cnt[_f] += 1
    TILE[_name] = (_i, _f, _cnt[_f])
UNIT_MID = {}
LAST_OF = {"g": (3,), "u": (3,), "d": (1, 3)}
_mid = 0
for _w, _u in enumerate(UNITS):
    if _u[0] == "ret":
        UNIT_TILE[_w] = TILE[("m", _w | 1)][0]
    elif _w < NMIX:
        UNIT_TILE[_w] = TILE[("m", _w)][0]
    elif _u[2] not in LAST_OF[_u[0]]:
        _mid += 1
        UNIT_MID[_w] = _mid
    elif _u[0] == "d":
        UNIT_TILE[_w] = TILE[("dn", _u[1], _u[2] // 2, _u[3])][0]
    else:
        UNIT_TILE[_w] = TILE[("h" + _u[0], _u[1], _u[3])][0]


SLOT, BEFORE, _last = {}, {}, {}
for _w in range(len(UNITS)):
    SLOT[_w] = _w % WS if _w < NMIX else (_w - NMIX) % ES
    if SLOT[_w] in _last:
        BEFORE[_w] = _last[SLOT[_w]]
    _last[SLOT[_w]] = _w


def build(nc, A, C, C2, O):
    f32, f32r = mybir.dt.float32, mybir.dt.float32r
    ALU, ACT, AX = mybir.AluOpType, mybir.ActivationFunctionType, mybir.AxisListType

    ctx = ExitStack()
    with ctx:
        def sb(name, shape, dt=f32):
            return ctx.enter_context(nc.sbuf_tensor(name, shape, dt))

        def sem(name):
            return ctx.enter_context(nc.semaphore(name))

        con = sb("con", [128, NCON])
        par_rows = sb("par_rows", [NPAR, 128])
        par = sb("par", [128, NPAR])
        cw = sb("cw", [128, KT, CW])
        wr = sb("wr", [128, KT, 20])
        br = sb("br", [20, 1])
        xT = sb("xT", [128, KT, T])
        h_hi = sb("h_hi", [128, KT, T], f32r)
        h_lo = sb("h_lo", [128, KT, T], f32r)
        raw = [sb(f"raw{i}", [128, 2048]) for i in range(WS)]
        w_hi = [sb(f"w_hi{i}", [128, 1024], f32r) for i in range(WS)]
        w_lo = [sb(f"w_lo{i}", [128, 1024], f32r) for i in range(WS)]
        sg = sb("sg", [128, 2, T])
        rstd = sb("rstd", [128, T])
        mixer = [("v_tok", [128, 3, NH * DV], f32), ("k_tok", [128, 2, 3, DK], f32), ("P", [128, 432], f32), ("osb", [128, DV], f32)]
        with ExitStack() as mx:
            def mo(sets):
                out, most = {}, 0
                for s in sets:
                    size = 0
                    with ExitStack() as inner:
                        for n, shape, dt in s:
                            out[n] = inner.enter_context(nc.sbuf_tensor(n, shape, dt))
                            size += -(-int(np.prod(shape[1:])) * 4 // 32) * 32
                    most = max(most, size)
                mx.enter_context(nc.sbuf_tensor(f"hold_{s[0][0]}", [128, most // 4], f32))
                return out

            R1 = mo([mixer, [("x_tok", [128, 3, D], f32), ("sc_rows", [120, 2, D], f32)],
                     [("on_hi", [128, ET, T], f32r), ("on_lo", [128, ET, T], f32r)],
                     [("m_hi", [128, KT, T], f32r), ("m_lo", [128, KT, T], f32r)]])
            R2 = mo([[("oT", [128, ET, T], f32)], [("stT", [128, KT, 240], f32), ("cw_rows", [CW, D], f32)],
                     [("yb", [128, KT, T], f32), ("ga", [128, KT, T], f32)]])
            R3 = mo([[("qT", [128, KT, T], f32), ("kT", [128, KT, T], f32)],
                     [("dummy_q", [128, KT, T], f32), ("sq0", [128, KT, T], f32)],
                     [("c_hi", [128, KT, T], f32r), ("c_lo", [128, KT, T], f32r)]])
            R4 = mo([[("conv", [128, KT, T], f32)], [("hf", [128, KT, T], f32)]])
            R5 = mo([[("S_ring", [128, 2, 2, 2, DV], f32)], [("ln_sq", [128, KT, T], f32)]])
            u = mx.enter_context(nc.sbuf_tensor("u", [128, KT, UW], f32))
            csamp = mx.enter_context(nc.sbuf_tensor("csamp", [128, KT, NSAMP], f32))
            R6 = mo([[("qk", [128, 2, 2, T], f32)], [("gsq", [128, 4, T], f32)]])
            R7 = mo([[("rot", [128, 2, 2, T], f32)], [("tg", [128, 2, T], f32), ("gstd", [128, T], f32)]])
            R8 = mo([[("vT", [128, 2, T], f32)], [("S_out", [128, 2, DV], f32)]])
            vT, S_out = R8["vT"], R8["S_out"]
            qm = mx.enter_context(nc.sbuf_tensor("qm", [128, KT, NSAMP, NSAMP], f32))
            utok = S_out
        with ExitStack() as me:
            def mt(name, shape, dt=f32):
                return me.enter_context(nc.sbuf_tensor(name, shape, dt))
            Y_hi = mt("Y_hi", [128, YS, D], f32r)
            Y_lo = mt("Y_lo", [128, YS, D], f32r)
            h2t_hi = mt("h2t_hi", [128, 3, D], f32r)
            h2t_lo = mt("h2t_lo", [128, 3, D], f32r)
            w_hi.append(mt("w_hi3", [128, 1024], f32r))
            w_lo.append(mt("w_lo3", [128, 1024], f32r))
            x_hi1 = mt("x_hi1", [128, 2, KT, CAP], f32r)
            x_lo1 = mt("x_lo1", [128, 2, KT, CAP], f32r)
            G = mt("G", [128, 3, 2, CAP], f32r)
            Gc = mt("Gc", [128, 2, 3, CAP])
            S_b = mt("S_b", [128, 2 * YS, T], f32r)
            cslot = mt("cslot", [128, NE])
            junk = mt("junk", [128, T])
            sgm = mt("sgm", [128, 2, DE])
            t_f = mt("t_f", [128, 2, DE])
            aT_hi = mt("aT_hi", [128, 4, CAP], f32r)
            aT_lo = mt("aT_lo", [128, 4, CAP], f32r)
            lgT = mt("lgT", [20, T])
            lg = mt("lg", [128, 3, 20])
            rt = mt("rt", [128, 3, 72])
            comb = mt("comb", [128, 3, NE])
            member = mt("member", [128, 3, NE])
            pos = mt("pos", [128, 3, NE])
            most = mt("most", [128, 2])
            most_i = mt("most_i", [128, 1], mybir.dt.int32)
            mcon = mt("mcon", [128, NMCON])
        with ExitStack() as me:
            m_size, y_size, x_at = 2 * KT * T, 2 * YS * D, 2 * YS * D + 2 * 3 * D + 2 * D
            me.enter_context(nc.sbuf_tensor("over_m", [128, m_size], f32))
            h2f = me.enter_context(nc.sbuf_tensor("h2f", [128, KT, T], f32))
            me.enter_context(nc.sbuf_tensor("to_x", [128, x_at - m_size - KT * T], f32))
            sq1 = me.enter_context(nc.sbuf_tensor("sq1", [128, KT, T], f32))
        with ExitStack() as me:
            y_tok = me.enter_context(nc.sbuf_tensor("y_tok", [128, 3, D], f32))
            sq2 = me.enter_context(nc.sbuf_tensor("sq2", [128, KT, T], f32))
            hfin = me.enter_context(nc.sbuf_tensor("hfin", [128, KT, T], f32))
        v_tok, k_tok, P, osb = R1["v_tok"], R1["k_tok"], R1["P"], R1["osb"]
        x_tok, sc_rows = R1["x_tok"], R1["sc_rows"]
        on_hi, on_lo, m_hi, m_lo = R1["on_hi"], R1["on_lo"], R1["m_hi"], R1["m_lo"]
        oT, stT, cw_rows, yb, ga = R2["oT"], R2["stT"], R2["cw_rows"], R2["yb"], R2["ga"]
        qT, kT, sq0, c_hi, c_lo = R3["qT"], R3["kT"], R3["sq0"], R3["c_hi"], R3["c_lo"]
        x_hi = [h_hi[:, :, :].rearrange("p k t -> p (k t)")[:, 0:2 * D].rearrange("p (e k c) -> p e k c", e=2, k=KT), x_hi1[:, :, :, :]]
        x_lo = [h_lo[:, :, :].rearrange("p k t -> p (k t)")[:, 0:2 * D].rearrange("p (e k c) -> p e k c", e=2, k=KT), x_lo1[:, :, :, :]]
        conv, hf, S_ring, ln_sq = R4["conv"], R4["hf"], R5["S_ring"], R5["ln_sq"]
        qk, gsq, rot, tg, gstd = R6["qk"], R6["gsq"], R7["rot"], R7["tg"], R7["gstd"]

        banks = [ctx.enter_context(nc.psum_tensor(f"bank{i}", [128, 512], f32)) for i in range(8)]
        o_samp = banks[7]

        def cst(name):
            at, k = CON[name]
            return con[:, at:at + k]

        ident = cst("ident")
        mask = cst("mask").rearrange("p (h i) -> p h i", h=NH)
        kdecay = cst("kdecay").rearrange("p (t h) -> p t h", t=3)
        eps = cst("eps")

        x_in, con_in, par_in, sc_in, cw_in, wr_in = (sem(n) for n in ("x_in", "con_in", "par_in", "sc_in", "cw_in", "wr_in"))
        raw_in = [sem(f"raw_in{i}") for i in range(WS)]
        S_in = [sem(f"S_in{i}") for i in range(2)]
        S_stored = [sem(f"S_stored{i}") for i in range(2)]
        Sp_stored = [sem(f"Sp_stored{i}") for i in range(2)]
        rows_stored, y_stored = sem("rows_stored"), sem("y_stored")
        hi_ready, lo_ready, unit_mid = sem("hi_ready"), sem("lo_ready"), sem("unit_mid")
        tile_ready = sem("tile_ready")
        act_freed, dve_freed = sem("act_freed"), sem("dve_freed")
        act_chain, dve_chain = sem("act_chain"), sem("dve_chain")
        S_used, S_scaled = sem("S_used"), sem("S_scaled")
        sig_ready, sq_ready, h_ready, hhi_ready, hlo_ready = (sem(n) for n in ("sig_ready", "sq_ready", "h_ready", "hhi_ready", "hlo_ready"))
        qk_ready, qm_ready, oc_ready, osq_ready, std_ready = (sem(n) for n in ("qk_ready", "qm_ready", "oc_ready", "osq_ready", "std_ready"))
        y_ready, yhi_ready, ylo_ready = sem("y_ready"), sem("yhi_ready"), sem("ylo_ready")
        m_ready, mhi_ready, mlo_ready = sem("m_ready"), sem("mhi_ready"), sem("mlo_ready")
        cc_ready, csq_ready, cz_ready, chi_ready, clo_ready, csig_ready = (sem(n) for n in ("cc_ready", "csq_ready", "cz_ready", "chi_ready", "clo_ready", "csig_ready"))
        conv_step, osb_ready, rot_ready, x2_ready = sem("conv_step"), sem("osb_ready"), sem("rot_ready"), sem("x2_ready")
        ex_ready, d_ready, member_ready, pos_ready, hthi_ready = (sem(n) for n in ("ex_ready", "d_ready", "member_ready", "pos_ready", "hthi_ready"))
        G_ready, Gc_ready, aThi_ready, yhi2_ready, ylo2_ready, sg2_ready, cslot_ready = (sem(n) for n in (
            "G_ready", "Gc_ready", "aThi_ready", "yhi2_ready", "ylo2_ready", "sg2_ready", "cslot_ready"))
        mcon_in, zero_ready = sem("mcon_in"), sem("zero_ready")
        fin_sq, fin_std, fin_h, fin_tile, fin_act, fin_dve = (sem(n) for n in ("fin_sq", "fin_std", "fin_h", "fin_tile", "fin_act", "fin_dve"))

        def bank(name):
            return banks[TILE[name][0] % BANKS]

        def seen(e, name):
            e.wait_ge(tile_ready, TILE[name][0] + 1)

        def evacuated(e, name):
            _, f, k = TILE[name]
            e.wait_ge(act_freed if f == "A" else dve_freed, k)

        def unit_used(e, w):
            if w in UNIT_MID:
                e.wait_ge(unit_mid, UNIT_MID[w])
            else:
                e.wait_ge(tile_ready, UNIT_TILE[w] + 1)

        def raw_view(w):
            s, m, r = UNITS[w][0], w % 2, raw[(w // 2) % WS]
            if s == "ret":
                return r[:, m * 1024:(m + 1) * 1024].rearrange("p (k n) -> p k n", k=8)
            if w >= NMIX:
                return r[:, m * 1024:(m + 1) * 1024].rearrange("p (k n) -> p k n", k=2)
            return r[:, :].rearrange("p (k n) -> p k n", k=8)[:, :, m * 128:(m + 1) * 128]

        def part_view(ring, w):
            return ring[SLOT[w]][:, :].rearrange("p (k n) -> p k n", k=2 if w >= NMIX else 8)

        def weights_of(c):
            un = UNITS[2 * c]
            s = un[0]
            cols = {"q": 2048, "k": 3072, "v": 4096, "glu_a": 0, "glu_b": 1024, "gret": 6144, "gate_a": 8192, "gate_b": 9216}
            if s in cols:
                at = cols[s] + un[1] * 128
                return A["w_in"][0].rearrange("(k p) n -> p k n", p=128)[:, :, at:at + 256], 8
            if s == "ret":
                at = un[1] // 2 * 128
                return A["w_ret_out"][0].rearrange("(k p) n -> p k n", p=128)[:, :, at:at + 128], 16
            if s in ("cout", "wo"):
                at = un[1] * 128
                return A["w_conv_out" if s == "cout" else "w_o"][0].rearrange("(k p) n -> p k n", p=128)[:, :, at:at + 256], 8
            if s in ("g", "u"):
                k = 2 * un[2]
                return A["w_gate_e" if s == "g" else "w_up_e"][0, un[1]].rearrange("(k p) n -> p k n", p=128)[:, k:k + 4, :], 4
            at = un[2] // 2 * 512
            return A["w_down_e"][0, un[1]].rearrange("(k p) n -> p k n", p=128)[:, :, at:at + 512], 4

        def later_rounds(e, body):
            count = e.value_load(most_i[0:1, 0:1], min_val=0, max_val=T)
            with e.If(count > CAP):
                body(1)
                with e.If(count > 2 * CAP):
                    body(2)
                e.nop()
            e.nop()

        def conv_quota(w):
            if GLU + 4 <= w < GRET:
                return 10
            if GRET <= w < GRET + 16:
                return 2
            if GRET + 16 <= w < GRET + 32:
                return 4
            if GRET + 32 <= w < FIRST["cout"] - 4:
                return 4
            return 0

        def dve_is_done(e):
            e.wait_ge(pos_ready, 1)

        block_1 = nc.Block()
        block = block_1.__enter__()

        @block.sync
        def _(sp):
            xs, meta = A["x_prompt"][0], A["meta_tokens"]
            n1 = 128 - NMETA
            sp.dma_start(x_tok[0:NMETA, 0, :], meta).then_inc(x_in, 16)
            sp.dma_start(x_tok[NMETA:128, 0, :], xs[0:n1]).then_inc(x_in, 16)
            sp.dma_start(x_tok[:, 1, :], xs[n1:n1 + 128]).then_inc(x_in, 16)
            sp.dma_start(x_tok[0:16, 2, :], xs[n1 + 128:SEQ]).then_inc(x_in, 16)
            sp.dma_start(x_tok[16:24, 2, :], A["x_sample"][:, 0, :]).then_inc(x_in, 16)
            def load_weights(c):
                if c >= WS:
                    sp.wait_ge(lo_ready, 2 * (c - WS) + 2)
                src, k = weights_of(c)
                sp.dma_start(raw[c % WS][:, :].rearrange("p (k n) -> p k n", k=k), src).then_inc(raw_in[c % WS], 16)
            for c in range((NMIX + PER_ROUND) // 2):
                load_weights(c)
            dve_is_done(sp)

            def more(r):
                for c in range((NMIX + r * PER_ROUND) // 2, (NMIX + (r + 1) * PER_ROUND) // 2):
                    load_weights(c)

            later_rounds(sp, more)

        @block.gpsimd
        def _(pool):
            pool.dma_start(cw_rows[:, :], A["conv_w"][0]).then_inc(cw_in, 16)
            for r in range(2):
                pool.dma_start(sc_rows[:, r, :], A["state_conv"][0, 4 * r:4 * r + 4].rearrange("b t d -> (b t) d")).then_inc(sc_in, 16)
            pool.dma_start(wr[:, :, 0:4], A["w_coarse"][0].rearrange("(k p) n -> p k n", p=128)).then_inc(wr_in, 16)
            pool.dma_start(wr[:, :, 4:20], A["w_fine"][0].rearrange("(k p) n -> p k n", p=128)).then_inc(wr_in, 16)
            pool.dma_start(br[0:4, :], A["b_coarse"][0].rearrange("(n a) -> n a", a=1)).then_inc(wr_in, 16)
            pool.dma_start(br[4:20, :], A["b_fine"][0].rearrange("(n a) -> n a", a=1)).then_inc(wr_in, 16)
            pool.dma_start(O["conv_sample"][0, :, 0:CW - 2, :], A["state_conv"][0, :, 1:CW - 1, :]).then_inc(rows_stored, 16)

            def load(s):
                h, b = s // 4, s % 4 * 2
                src = A["state_ret"][0, b:b + 2, h].rearrange("b (t p) e -> p b t e", p=128)
                for i in range(2):
                    pool.dma_start(S_ring[:, s % 2, i], src[:, i]).then_inc(S_in[s % 2], 16)

            def store(s):
                h, b = s // 4, s % 4 * 2
                dst = O["ret_sample"][0, b:b + 2, h].rearrange("b (t p) e -> p b t e", p=128)
                evacuated(pool, ("vb", s, 1))
                for i in range(2):
                    pool.dma_start(dst[:, i], S_ring[:, s % 2, i]).then_inc(S_stored[s % 2], 16)

            load(0)
            load(1)
            for s in range(16):
                if s >= 1 and s <= NH:
                    h = s - 1
                    for dt in range(2):
                        evacuated(pool, ("S", h, dt))
                        pool.dma_start(O["ret_prompt"][0, 0, h, dt * 128:(dt + 1) * 128, :], S_out[:, dt, :]).then_inc(Sp_stored[dt], 16)
                store(s)
                if s + 2 < 16:
                    pool.wait_ge(S_stored[s % 2], 32 * (s // 2 + 1))
                    pool.wait_ge(S_used, s + 1)
                    load(s + 2)
            seen(pool, ("m", NMIX - 1))
            evacuated(pool, ("m", NMIX - 1))
            pool.memset(h2t_hi[:, 2, :].bitcast(f32), 0.0).then_inc(zero_ready, 1)
            pool.memset(h2t_lo[:, 2, :].bitcast(f32), 0.0).then_inc(zero_ready, 1)
            pool.dma_start(mcon[:, :], C2).then_inc(mcon_in, 16)
            evacuated(pool, ("ut", 1))
            ut = utok[0:PAD + NSAMP, :, :].rearrange("p a b -> p (a b)")
            pool.dma_start(O["conv_prompt"][0, 0], ut[0:PAD, :]).then_inc(rows_stored, 16)
            pool.dma_start(O["conv_sample"][0, :, CW - 2, :], ut[PAD:PAD + NSAMP, :]).then_inc(rows_stored, 16)

        @block.scalar
        def _(act):
            n = {"chain": 0}

            def link(ins):
                n["chain"] += 1
                ins.then_inc(act_chain, 1)
                act.wait_ge(act_chain, n["chain"])

            def hi(w):
                if w >= len(UNITS):
                    return
                if w % 2 == 0:
                    act.wait_ge(raw_in[(w // 2) % WS], 16 * (w // 2 // WS + 1))
                if w in BEFORE:
                    unit_used(act, BEFORE[w])
                act.activation(part_view(w_hi, w), raw_view(w), ACT.Copy).then_inc(hi_ready, 1)

            def free(ins):
                ins.then_inc(act_freed, 1)

            act.dma_start(con[:, :], C).then_inc(con_in, 16)
            at = 0
            for name in ("norm_mix_g", "b_gates", "conv_b", "conv_ln_g", "conv_ln_b", "ret_gn_g", "norm_ffn_g"):
                v = A[name][0].rearrange("(k p) -> k p", p=128)
                act.dma_start(par_rows[at:at + v.shape[0], :], v).then_inc(par_in, 16)
                at += v.shape[0]
            act.dma_start(par_rows[at:at + 8, :], A["norm_final_g"].rearrange("(k p) -> k p", p=128)).then_inc(par_in, 16)
            for tt, (t0, nt) in enumerate(TOKENS):
                seen(act, ("xt", tt, 0))
                src = bank(("xt", tt, 0))[:, :].rearrange("p (f n) -> p f n", f=4)[:, :, 0:nt]
                free(act.activation(xT[:, 0:4, t0:t0 + nt], src, ACT.Copy))
            evacuated(act, ("xt", 2, 0))
            act.activation(sq0[:, 0:4, :], xT[:, 0:4, :], ACT.Square).then_inc(sq_ready, 1)
            evacuated(act, ("xt", 2, 1))
            act.activation(sq0[:, 4:8, :], xT[:, 4:8, :], ACT.Square).then_inc(sq_ready, 1)

            def norm_act(i, hsrc):
                seen(act, ("norm", i))
                if i == 0:
                    act.wait_ge(con_in, 16)
                ins = act.activation(rstd[:, :], bank(("norm", i))[:, 0:T], ACT.Sqrt, bias=eps)
                free(ins)
                if i < 2:
                    for k in range(2):
                        act.wait_ge(h_ready, 2 * i + k + 1)
                        act.activation(h_hi[:, 4 * k:4 * k + 4, :], hsrc[:, 4 * k:4 * k + 4, :], ACT.Copy).then_inc(hhi_ready, 1)

            hi(0)
            norm_act(0, hf)
            hi(1)

            for w in range(NMIX):
                s, i = UNITS[w]
                hi(w + 2)
                if w > GRET and w <= GRET + 16:
                    f = w - 1 - GRET
                    act.wait_ge(y_ready, f + 1)
                    act.activation(on_hi[:, f, :], oT[:, f, :], ACT.Copy).then_inc(yhi_ready, 1)
                if w > FIRST["cout"] and w <= FIRST["cout"] + 8:
                    f = w - 1 - FIRST["cout"]
                    act.wait_ge(m_ready, f + 1)
                    act.activation(m_hi[:, f, :], yb[:, f, :], ACT.Copy).then_inc(mhi_ready, 1)
                if s in ("q", "k"):
                    p = (0 if s == "q" else 4) + i // 2
                    if i % 2 == 0 and p >= 2:
                        act.wait_ge(rot_ready, p - 1)
                    seen(act, ("m", w))
                    free(act.activation(qk[:, p % 2, i % 2, :], bank(("m", w))[:, 0:T], ACT.Copy,
                                        scale=1.0 if s == "q" else DK ** -0.5))
                if s == "v":
                    if i >= 2:
                        seen(act, ("vt", i - 2))
                    seen(act, ("m", w))
                    free(act.activation(vT[:, i % 2, :], bank(("m", w))[:, 0:T], ACT.Copy))
                if s == "glu_b":
                    if i >= 2:
                        evacuated(act, ("m", w - 2))
                    seen(act, ("m", w))
                    free(act.activation(sg[:, i % 2, :], bank(("m", w))[:, 0:T], ACT.Sigmoid))
                if s == "gret":
                    g = i
                    if g >= 2:
                        evacuated(act, ("m", w - 2))
                    seen(act, ("m", w))
                    act.activation(sg[:, g % 2, :], bank(("m", w))[:, 0:T], ACT.Sigmoid).then_inc(sig_ready, 1)
                if s == "ret" and i % 2 == 1:
                    seen(act, ("m", w))
                    if i == 1:
                        act.wait_ge(ylo_ready, ET)
                    free(act.activation(yb[:, i // 2, :], bank(("m", w))[:, 0:T], ACT.Copy))
                if s == "gate_b":
                    if i >= 2:
                        evacuated(act, ("m", w - 2))
                    seen(act, ("m", w))
                    act.activation(sg[:, i % 2, :], bank(("m", w))[:, 0:T], ACT.Sigmoid,
                                   bias=par[:, PAR["b_gates"] + 8 + i:PAR["b_gates"] + 9 + i]).then_inc(sig_ready, 1)
                if s == "gate_a":
                    seen(act, ("m", w))
                    free(act.activation(ga[:, i, :], bank(("m", w))[:, 0:T], ACT.Sigmoid,
                                        bias=par[:, PAR["b_gates"] + i:PAR["b_gates"] + 1 + i]))
                if 2 <= w < 6:
                    r, hf2 = (w - 2) // 2, w % 2
                    seen(act, ("sc", r, hf2))
                    free(act.activation(stT[:, 4 * hf2:4 * hf2 + 4, r * 120:(r + 1) * 120],
                                        bank(("sc", r, hf2))[:, 0:480].rearrange("p (f n) -> p f n", f=4), ACT.Copy))
                if GLU <= w < EXTRA_END:
                    k = w - GLU
                    if k == 0:
                        act.wait_ge(qm_ready, 1)
                    if k < NH:
                        for tt in range(3):
                            nt = min(128, TP - TOKENS[tt][0])
                            nm = ("kt", k, 0 if tt < 2 else 1)
                            if tt == 0 and k >= 2:
                                seen(act, ("S", k - 2, 1))
                            seen(act, nm)
                            col = tt * DK if tt < 2 else 0
                            ins = act.activation(k_tok[0:nt, k % 2, tt, :], bank(nm)[0:nt, col:col + DK], ACT.Copy,
                                                 scale=kdecay[0:nt, tt, k:k + 1])
                            if tt:
                                free(ins)
                    if 1 <= k <= NH:
                        h = k - 1
                        for et in range(4):
                            seen(act, ("o", h, et))
                            free(act.activation(oT[:, 4 * h + et, 0:TP], bank(("o", h, et))[:, 0:TP], ACT.Copy))
                        for dt in range(2):
                            seen(act, ("S", h, dt))
                            if h >= 1:
                                act.wait_ge(Sp_stored[dt], 16 * h)
                            free(act.activation(S_out[:, dt, :], bank(("S", h, dt))[:, :], ACT.Copy))
                    if k >= 4 and k % 4 == 0 and k <= 16:
                        h = k // 4 - 1
                        act.wait_ge(S_used, 4 * h + 4)
                        if h >= 1:
                            seen(act, ("ot", h - 1))
                        for q in range(4):
                            ins = act.activation(osb[32 * q:32 * q + NSAMP, :], o_samp[32 * q:32 * q + NSAMP, :], ACT.Copy)
                        ins.then_inc(osb_ready, 1)
                    if k >= 5 and (k - 5) % 4 == 0 and k <= 17:
                        h = (k - 5) // 4
                        seen(act, ("ot", h))
                        free(act.activation(oT[:, 4 * h:4 * h + 4, TP:T],
                                            bank(("ot", h))[:, 0:32].rearrange("p (f n) -> p f n", f=4), ACT.Copy))
                    if k >= 6 and (k - 6) % 4 == 0 and k <= 18:
                        h = (k - 6) // 4
                        evacuated(act, ("gm", h))
                        if h >= 1:
                            seen(act, ("gv", h - 1))
                        act.activation(gsq[:, :, :], oT[:, 4 * h:4 * h + 4, :], ACT.Square).then_inc(osq_ready, 1)
                    if k >= 7 and (k - 7) % 4 == 0 and k <= 19:
                        h = (k - 7) // 4
                        seen(act, ("gv", h))
                        if h >= 1:
                            act.wait_ge(std_ready, h)
                        free(act.activation(gstd[:, :], bank(("gv", h))[:, 0:T], ACT.Sqrt, bias=eps))
                    if k in (20, 21):
                        q = k - 20
                        if q == 0:
                            act.wait_ge(Sp_stored[0], 16 * NH)
                            act.wait_ge(Sp_stored[1], 16 * NH)
                        seen(act, ("ut", q))
                        free(act.activation(utok[0:PAD + NSAMP, q, :], bank(("ut", q))[0:PAD + NSAMP, :], ACT.Copy))
                if GLU - 1 <= w < GRET - 1:
                    s2 = w - GLU + 1
                    act.wait_ge(S_in[s2 % 2], 32 * (s2 // 2 + 1))
                    v = S_ring[:, s2 % 2].rearrange("p b t e -> p (b t e)")
                    act.activation(v, v, ACT.Copy, scale=GAMMA[s2 // 4]).then_inc(S_scaled, 1)
                if w == FIRST["cout"] - 4:
                    evacuated(act, ("lm",))
                    for j in range(2):
                        act.wait_ge(S_stored[j], 16 * 16)
                    act.activation(ln_sq[:, :, :], conv[:, :, :], ACT.Square).then_inc(csq_ready, 1)
                if w == FIRST["cout"] - 3:
                    seen(act, ("lv",))
                    free(act.activation(rstd[:, :], bank(("lv",))[:, 0:T], ACT.Sqrt, bias=eps))
                if w == FIRST["cout"] - 2:
                    act.wait_ge(cz_ready, 1)
                    for f in range(KT):
                        g = par[:, PAR["ln_g"] + f:PAR["ln_g"] + f + 1]
                        b = par[:, PAR["ln_b"] + f:PAR["ln_b"] + f + 1]
                        act.activation(ln_sq[:, f, :], conv[:, f, :], ACT.Sigmoid, scale=g, bias=b).then_inc(csig_ready, 1)
                if w == FIRST["cout"] - 1:
                    for f in range(KT):
                        act.wait_ge(cz_ready, 2 + f)
                        act.activation(c_hi[:, f, :], conv[:, f, :], ACT.Copy).then_inc(chi_ready, 1)

            for k in range(2):
                evacuated(act, ("m", FIRST["wo"] + 4 * k + 3))
                act.activation(sq1[:, 4 * k:4 * k + 4, :], xT[:, 4 * k:4 * k + 4, :], ACT.Square).then_inc(sq_ready, 1)
            seen(act, ("norm", 1))
            free(act.activation(rstd[:, :], bank(("norm", 1))[:, 0:T], ACT.Sqrt, bias=eps))
            act.wait_ge(wr_in, 64)
            seen(act, ("logit",))
            free(act.activation(lgT[:, :], bank(("logit",))[0:20, 0:T], ACT.Identity, bias=br[:, 0:1]))
            act.wait_ge(zero_ready, 2)
            for tt, (t0, nt) in enumerate(TOKENS):
                for hf2 in range(2):
                    seen(act, ("ht", tt, hf2))
                    act.activation(h2t_hi[0:nt, tt, hf2 * 512:(hf2 + 1) * 512], bank(("ht", tt, hf2))[0:nt, :], ACT.Copy).then_inc(hthi_ready, 1)
            act.wait_ge(ex_ready, 1)
            act.activation(rt[:, :, 0:4], rt[:, :, 0:4], ACT.Exp).then_inc(ex_ready, 1)
            act.wait_ge(d_ready, 1)
            act.activation(rt[:, :, 8:9], rt[:, :, 8:9], ACT.Exp).then_inc(d_ready, 1)

            def x_tiles(p, js, rd):
                for j in js:
                    seen(act, ("x", p, j, rd))
                    dst = (x_hi if j < 4 else x_lo)[p % 2]
                    src = bank(("x", p, j, rd))[:, :].rearrange("p (k e c) -> p e k c", k=2, e=2)
                    k = 2 * (j % 4)
                    free(act.activation(dst[:, :, k:k + 2, :], src, ACT.Copy))

            def experts_act(rd):
                base = NMIX + rd * PER_ROUND
                for i in range(0 if rd else 2, LOOK):
                    hi(base + i)
                x_tiles(0, range(8), rd)
                w = base
                n_e = rd * NE
                for e in range(NE + 1):
                    if e < NE:
                        for _ in range(4):
                            if w + LOOK < base + PER_ROUND:
                                hi(w + LOOK)
                            w += 1
                        g = n_e + e
                        if e >= 2 or rd:
                            act.wait_ge(dve_freed, TILE[hg_before(e, rd)][2])
                        seen(act, ("hg", e, rd))
                        act.activation(sgm[:, e % 2, :], bank(("hg", e, rd))[:, :], ACT.Sigmoid).then_inc(sg2_ready, 1)
                    if e > 0:
                        seen(act, ("tr", e - 1, rd))
                        if e > 1 or rd:
                            unit_used(act, UNIT[("d", (e - 2) % NE, 3, rd if e > 1 else rd - 1)])
                        act.activation(aT_hi[:, :, :], bank(("tr", e - 1, rd))[:, :].rearrange("p (k c) -> p k c", k=4),
                                       ACT.Copy).then_inc(aThi_ready, 1)
                    if e < NE:
                        seen(act, ("st", e, rd))
                        b = bank(("st", e, rd))[:, 0:T]
                        if e >= 1 or rd:
                            act.wait_ge(cslot_ready, n_e + e)
                        act.activation(junk[:, :], b, ACT.Copy, accum_out=cslot[:, e:e + 1]).then_inc(cslot_ready, 1)
                        free(act.activation(S_b[:, e % (2 * YS), :], b, ACT.Sign))
                        if e // 2 + 1 < NE // 2:
                            x_tiles(e // 2 + 1, range(4 * (e % 2), 4 * (e % 2) + 4), rd)
                        for _ in range(4):
                            if w + LOOK < base + PER_ROUND:
                                hi(w + LOOK)
                            w += 1
                    if e > 0:
                        act.wait_ge(cslot_ready, n_e + e)
                        for j in range(2):
                            for _ in range(2):
                                if w + LOOK < base + PER_ROUND:
                                    hi(w + LOOK)
                                w += 1
                            seen(act, ("dn", e - 1, j, rd))
                            act.activation(Y_hi[:, (e - 1) % YS, j * 512:(j + 1) * 512], bank(("dn", e - 1, j, rd))[:, :], ACT.Copy,
                                           scale=cslot[:, e - 1:e]).then_inc(yhi2_ready, 1)

            experts_act(0)
            dve_is_done(act)
            later_rounds(act, experts_act)

        @block.vector
        def _(dve):
            n = {"chain": 0, "conv": 0, "u": -1}

            def link(ins):
                n["chain"] += 1
                ins.then_inc(dve_chain, 1)
                dve.wait_ge(dve_chain, n["chain"])

            def free(ins):
                ins.then_inc(dve_freed, 1)

            def lo(w):
                if w >= len(UNITS):
                    return
                dve.wait_ge(hi_ready, w + 1)
                dve.tensor_tensor(part_view(w_lo, w), raw_view(w), part_view(w_hi, w).bitcast(f32), ALU.subtract).then_inc(lo_ready, 1)

            convs = []
            for p in range(4):
                for t in range(CW):
                    convs += [(2 * p, t), (2 * p + 1, t)]

            def conv_steps(k):
                for _ in range(k):
                    c = n["conv"]
                    if c >= len(convs):
                        return
                    f, t = convs[c]
                    if f > n["u"]:
                        return
                    n["conv"] += 1
                    w_t = cw[:, f, t:t + 1]
                    out, src = conv[:, f, 0:TP], u[:, f, t:t + TP]
                    if t == 0:
                        dve.tensor_scalar(out, src, w_t, par[:, PAR["conv_b"] + f:PAR["conv_b"] + f + 1],
                                          ALU.mult, ALU.add).then_inc(conv_step, 1)
                    else:
                        dve.wait_ge(conv_step, c - 1)
                        dve.scalar_tensor_tensor(out=out, in0=src, scalar=w_t, in1=out, op0=ALU.mult,
                                                 op1=ALU.add).then_inc(conv_step, 1)

            dve.memset(u[:, :, 0:PAD], 0.0)
            for tt, (t0, nt) in enumerate(TOKENS):
                seen(dve, ("xt", tt, 1))
                src = bank(("xt", tt, 1))[:, :].rearrange("p (f n) -> p f n", f=4)[:, :, 0:nt]
                free(dve.tensor_copy(xT[:, 4:8, t0:t0 + nt], src))
            seen(dve, ("par",))
            free(dve.tensor_copy(par[:, :], bank(("par",))[:, 0:NPAR]))

            def norm_dve(i, name, dst):
                evacuated(dve, ("norm", i))
                link(dve.reciprocal(rstd[:, :], rstd[:, :]))
                for f in range(KT):
                    g = par[:, PAR[name] + f:PAR[name] + f + 1]
                    ins = dve.scalar_tensor_tensor(out=dst[:, f, :], in0=xT[:, f, :], scalar=g, in1=rstd[:, :],
                                                   op0=ALU.mult, op1=ALU.mult)
                    if f % 4 == 3:
                        ins.then_inc(h_ready, 1)
                for k in range(2):
                    dve.wait_ge(hhi_ready, 2 * i + k + 1)
                    sl = slice(4 * k, 4 * k + 4)
                    dve.tensor_tensor(h_lo[:, sl, :], dst[:, sl, :], h_hi[:, sl, :].bitcast(f32), ALU.subtract).then_inc(hlo_ready, 1)

            lo(0)
            evacuated(dve, ("par",))
            norm_dve(0, "norm_mix", hf)
            lo(1)
            cos2 = cst("cos").rearrange("p (a t) -> p a t", a=1).broadcast_to([128, 2, T])
            sin2 = cst("sin").rearrange("p (a t) -> p a t", a=1).broadcast_to([128, 2, T])

            for w in range(NMIX):
                s, i = UNITS[w]
                lo(w + 2)
                if w > GRET and w <= GRET + 16:
                    f = w - 1 - GRET
                    dve.wait_ge(yhi_ready, f + 1)
                    dve.tensor_tensor(on_lo[:, f, :], oT[:, f, :], on_hi[:, f, :].bitcast(f32), ALU.subtract).then_inc(ylo_ready, 1)
                if w > FIRST["cout"] and w <= FIRST["cout"] + 8:
                    f = w - 1 - FIRST["cout"]
                    dve.wait_ge(mhi_ready, f + 1)
                    dve.tensor_tensor(m_lo[:, f, :], yb[:, f, :], m_hi[:, f, :].bitcast(f32), ALU.subtract).then_inc(mlo_ready, 1)
                if s in ("q", "k") and i % 2 == 1:
                    p = (0 if s == "q" else 4) + i // 2
                    dst = qT if s == "q" else kT
                    evacuated(dve, ("m", w))
                    if p >= 1:
                        dve.wait_ge(rot_ready, p)
                    dve.tensor_tensor(rot[:, 0, :, :], qk[:, p % 2, :, :], cos2, ALU.mult)
                    link(dve.tensor_tensor(rot[:, 1, :, :], qk[:, p % 2, :, :], sin2, ALU.mult))
                    dve.tensor_tensor(dst[:, i - 1, :], rot[:, 0, 0, :], rot[:, 1, 1, :], ALU.subtract)
                    dve.tensor_tensor(dst[:, i, :], rot[:, 1, 0, :], rot[:, 0, 1, :], ALU.add).then_inc(rot_ready, 1)
                if s == "glu_a":
                    evacuated(dve, ("m", w - 2))
                    seen(dve, ("m", w))
                    free(dve.tensor_tensor(u[:, i, PAD:UW], bank(("m", w))[:, 0:T], sg[:, i % 2, :], ALU.mult))
                    n["u"] = 2 * (i // 2) - 1 if i % 2 == 0 else i
                if s == "gret":
                    seen(dve, ("m", w))
                    dve.wait_ge(sig_ready, i + 1)
                    if i >= 1:
                        dve.wait_ge(y_ready, i)
                    ins = dve.tensor_tensor(tg[:, i % 2, :], bank(("m", w))[:, 0:T], sg[:, i % 2, :], ALU.mult)
                    free(ins)
                    evacuated(dve, ("m", w))
                    g = par[:, PAR["gn_g"] + i:PAR["gn_g"] + i + 1]
                    dve.scalar_tensor_tensor(out=oT[:, i, :], in0=oT[:, i, :], scalar=g, in1=tg[:, i % 2, :],
                                             op0=ALU.mult, op1=ALU.mult).then_inc(y_ready, 1)
                if s == "gate_b":
                    evacuated(dve, ("m", FIRST["ret"] + 2 * i + 1))
                    dve.wait_ge(sig_ready, 16 + i + 1)
                    free(dve.tensor_tensor(yb[:, i, :], yb[:, i, :], sg[:, i % 2, :], ALU.mult))
                if s == "cout":
                    seen(dve, ("m", w))
                    evacuated(dve, ("m", FIRST["gate_a"] + i))
                    free(dve.tensor_tensor(ga[:, i, :], bank(("m", w))[:, 0:T], ga[:, i, :], ALU.mult))
                    evacuated(dve, ("m", w))
                    dve.tensor_tensor(yb[:, i, :], yb[:, i, :], ga[:, i, :], ALU.add).then_inc(m_ready, 1)
                if s == "wo":
                    seen(dve, ("m", w))
                    ins = dve.tensor_tensor(xT[:, i, :], bank(("m", w))[:, 0:T], xT[:, i, :], ALU.add)
                    free(ins)
                if w == 1:
                    seen(dve, ("cw",))
                    free(dve.tensor_copy(cw[:, :, :], bank(("cw",))[:, 0:KT * CW].rearrange("p (f t) -> p f t", f=KT)))
                if w in (6, 7):
                    if w == 6:
                        evacuated(dve, ("sc", 1, 1))
                        evacuated(dve, ("cw",))
                    for f in range(4 * (w - 6), 4 * (w - 6) + 4):
                        wb = cw[:, f:f + 1, 0:CW - 1].broadcast_to([128, NSAMP, CW - 1])
                        v = stT[:, f, :].rearrange("p (b t) -> p b t", b=NSAMP)
                        last = dve.tensor_tensor(v, v, wb, ALU.mult)
                    link(last)
                    sl = slice(4 * (w - 6), 4 * (w - 6) + 4)
                    link(dve.tensor_reduce(out=csamp[:, sl, :], in_=stT[:, sl, :].rearrange("p f (b t) -> p f b t", b=NSAMP),
                                      axis=AX.X, op=ALU.add))
                    for f in range(4 * (w - 6), 4 * (w - 6) + 4):
                        last = dve.tensor_scalar(csamp[:, f, :], csamp[:, f, :], par[:, PAR["conv_b"] + f:PAR["conv_b"] + f + 1],
                                                 None, ALU.add)
                    link(last)
                if FIRST["v"] < w <= FIRST["v"] + 16:
                    j = w - 1 - FIRST["v"]
                    seen(dve, ("vt", j))
                    b = bank(("vt", j))
                    dve.tensor_copy(v_tok[:, 0:2, j * 128:(j + 1) * 128], b[:, 0:256].rearrange("p (t n) -> p t n", t=2))
                    free(dve.tensor_copy(v_tok[0:24, 2, j * 128:(j + 1) * 128], b[0:24, 256:384]))
                if w == FIRST["v"]:
                    dve.wait_ge(rot_ready, 8)
                    dve.memset(v_tok[:, 2, :], 0.0)
                    dve.memset(k_tok[:, :, 2, :], 0.0)
                    dve.memset(osb[:, :], 0.0)
                    link(dve.memset(qm[:, :, :, :], 0.0))
                    for b in range(NSAMP):
                        last = dve.tensor_copy(qm[:, :, b, b:b + 1], qT[:, :, TP + b:TP + b + 1])
                    last.then_inc(qm_ready, 1)
                if GLU <= w < EXTRA_END:
                    k = w - GLU
                    if k < NH:
                        if k >= 1:
                            seen(dve, ("o", k - 1, 3))
                        seen(dve, ("score", k))
                        b = bank(("score", k))
                        dve.tensor_tensor(P[:, 0:272], b[:, 0:272], mask[:, k, 0:272], ALU.mult)
                        dve.tensor_tensor(P[:, 272:416], b[:, 272:416], mask[:, k, 0:144], ALU.mult)
                        free(dve.tensor_tensor(P[0:16, 416:432], b[0:16, 416:432], mask[0:16, k, 0:16], ALU.mult))
                    if k < 16:
                        h = k // 4
                        dve.wait_ge(S_scaled, k + 1)
                        for j in range(2):
                            smp = 2 * (k % 4) + j
                            seen(dve, ("vb", k, j))
                            for dt in range(2):
                                st = S_ring[:, k % 2, j, dt, :]
                                f = 2 * h + dt
                                ins = dve.scalar_tensor_tensor(out=st, in0=bank(("vb", k, j))[:, :],
                                                               scalar=kT[:, f, TP + smp:TP + smp + 1], in1=st,
                                                               op0=ALU.mult, op1=ALU.add)
                            free(ins)
                    if k >= 6 and (k - 6) % 4 == 0 and k <= 18:
                        h = (k - 6) // 4
                        seen(dve, ("gm", h))
                        evacuated(dve, ("ot", h))
                        mb = bank(("gm", h))[:, 0:T].rearrange("p (a t) -> p a t", a=1).broadcast_to([128, 4, T])
                        v = oT[:, 4 * h:4 * h + 4, :]
                        free(dve.tensor_tensor(v, v, mb, ALU.subtract))
                    if k >= 7 and (k - 7) % 4 == 0 and k <= 19:
                        h = (k - 7) // 4
                        evacuated(dve, ("gv", h))
                        link(dve.reciprocal(rstd[:, :], gstd[:, :]))
                        rb = rstd[:, :].rearrange("p (a t) -> p a t", a=1).broadcast_to([128, 4, T])
                        v = oT[:, 4 * h:4 * h + 4, :]
                        dve.wait_ge(osq_ready, h + 1)
                        dve.tensor_tensor(v, v, rb, ALU.mult).then_inc(std_ready, 1)
                        dve.wait_ge(std_ready, h + 1)
                conv_steps(conv_quota(w))
                if w == FIRST["cout"] - 5:
                    conv_steps(len(convs))
                    for f in range(KT):
                        last = dve.scalar_tensor_tensor(out=conv[:, f, TP:T], in0=u[:, f, PAD + TP:UW], scalar=cw[:, f, CW - 1:CW],
                                                        in1=csamp[:, f, :], op0=ALU.mult, op1=ALU.add)
                    last.then_inc(conv_step, 1)
                if w == FIRST["cout"] - 4:
                    seen(dve, ("lm",))
                    mb = bank(("lm",))[:, 0:T].rearrange("p (a t) -> p a t", a=1).broadcast_to([128, KT, T])
                    free(dve.tensor_tensor(conv[:, :, :], conv[:, :, :], mb, ALU.subtract))
                if w == FIRST["cout"] - 3:
                    evacuated(dve, ("lv",))
                    link(dve.reciprocal(rstd[:, :], rstd[:, :]))
                    rb = rstd[:, :].rearrange("p (a t) -> p a t", a=1).broadcast_to([128, KT, T])
                    dve.wait_ge(csq_ready, 1)
                    dve.tensor_tensor(conv[:, :, :], conv[:, :, :], rb, ALU.mult).then_inc(cz_ready, 1)
                    dve.wait_ge(cz_ready, 1)
                if w == FIRST["cout"] - 1:
                    for f in range(KT):
                        g = par[:, PAR["ln_g"] + f:PAR["ln_g"] + f + 1]
                        b = par[:, PAR["ln_b"] + f:PAR["ln_b"] + f + 1]
                        dve.wait_ge(csig_ready, f + 1)
                        link(dve.tensor_scalar(conv[:, f, :], conv[:, f, :], g, b, ALU.mult, ALU.add))
                        dve.tensor_tensor(conv[:, f, :], conv[:, f, :], ln_sq[:, f, :], ALU.mult).then_inc(cz_ready, 1)
                    for f in range(KT):
                        dve.wait_ge(chi_ready, f + 1)
                        dve.tensor_tensor(c_lo[:, f, :], conv[:, f, :], c_hi[:, f, :].bitcast(f32), ALU.subtract).then_inc(clo_ready, 1)

            evacuated(dve, ("norm", 1))
            link(dve.reciprocal(rstd[:, :], rstd[:, :]))
            for f in range(KT):
                g = par[:, PAR["norm_ffn"] + f:PAR["norm_ffn"] + f + 1]
                dve.scalar_tensor_tensor(out=h2f[:, f, :], in0=xT[:, f, :], scalar=g, in1=rstd[:, :],
                                         op0=ALU.mult, op1=ALU.mult).then_inc(h_ready, 1)
            for tt, (t0, nt) in enumerate(TOKENS):
                for hf2 in range(2):
                    dve.wait_ge(hthi_ready, 2 * tt + hf2 + 1)
                    sl = slice(hf2 * 512, (hf2 + 1) * 512)
                    free(dve.tensor_tensor(h2t_lo[0:nt, tt, sl], bank(("ht", tt, hf2))[0:nt, :], h2t_hi[0:nt, tt, sl].bitcast(f32),
                                           ALU.subtract))
            link(dve.memset(lg[:, :, :], 0.0))
            seen(dve, ("lt",))
            b = bank(("lt",))
            dve.tensor_copy(lg[:, 0:2, :], b[:, 0:40].rearrange("p (t n) -> p t n", t=2))
            free(dve.tensor_copy(lg[0:24, 2, :], b[0:24, 40:60]))
            evacuated(dve, ("lt",))
            rank = cst("rank").rearrange("p (a k) -> p a k", a=1).broadcast_to([128, 3, 4])
            L4, F16 = lg[:, :, 0:4], lg[:, :, 4:20]
            ex, mx4, og, o1, o2, tmp = rt[:, :, 0:4], rt[:, :, 12:13], rt[:, :, 16:20], rt[:, :, 20:24], rt[:, :, 24:28], rt[:, :, 28:32]
            dd, v1, v2, pg, w1, w2, sel = rt[:, :, 8:9], rt[:, :, 9:10], rt[:, :, 10:11], rt[:, :, 11:12], rt[:, :, 13:14], rt[:, :, 14:15], rt[:, :, 32:36]
            prod = rt[:, :, 48:64]

            def bc(x, k=4):
                return x.broadcast_to([128, 3, k])

            def first_max(out, src, top):
                link(dve.tensor_tensor(tmp, src, bc(top), ALU.is_equal))
                link(dve.tensor_tensor(tmp, tmp, rank, ALU.mult))
                link(dve.tensor_reduce(out=w2, in_=tmp, axis=AX.X, op=ALU.max))
                link(dve.tensor_tensor(out, tmp, bc(w2), ALU.is_equal))

            link(dve.tensor_reduce(out=mx4, in_=L4, axis=AX.X, op=ALU.max))
            dve.tensor_tensor(ex, L4, bc(mx4), ALU.subtract).then_inc(ex_ready, 1)
            first_max(og, L4, mx4)
            link(dve.tensor_tensor(prod.rearrange("p t (g i) -> p t g i", g=4), F16.rearrange("p t (g i) -> p t g i", g=4),
                                   og.rearrange("p t (g a) -> p t g a", a=1).broadcast_to([128, 3, 4, 4]), ALU.mult))
            link(dve.tensor_reduce(out=sel, in_=prod.rearrange("p t (g i) -> p t i g", g=4), axis=AX.X, op=ALU.add))
            link(dve.tensor_reduce(out=v1, in_=sel, axis=AX.X, op=ALU.max))
            first_max(o1, sel, v1)
            link(dve.scalar_tensor_tensor(out=sel, in0=o1, scalar=-3.0e38, in1=sel, op0=ALU.mult, op1=ALU.add))
            link(dve.tensor_reduce(out=v2, in_=sel, axis=AX.X, op=ALU.max))
            first_max(o2, sel, v2)
            dve.tensor_tensor(dd, v2, v1, ALU.subtract).then_inc(d_ready, 1)
            o12 = rt[:, :, 64:68]
            link(dve.tensor_tensor(o12, o1, o2, ALU.add))

            def by_group(out, x):
                return dve.tensor_tensor(out[:, :, :].rearrange("p t (g i) -> p t g i", g=4),
                                         og.rearrange("p t (g a) -> p t g a", a=1).broadcast_to([128, 3, 4, 4]),
                                         x.rearrange("p t (a i) -> p t a i", a=1).broadcast_to([128, 3, 4, 4]), ALU.mult)

            by_group(member, o12).then_inc(member_ready, 1)
            dve.wait_ge(ex_ready, 2)
            link(dve.tensor_reduce(out=pg, in_=ex, axis=AX.X, op=ALU.add))
            link(dve.reciprocal(pg, pg))
            dve.wait_ge(d_ready, 2)
            link(dve.tensor_scalar(w1, dd, 1.0, None, ALU.add))
            link(dve.reciprocal(w1, w1))
            link(dve.tensor_tensor(w1, w1, pg, ALU.mult))
            link(dve.tensor_tensor(w2, w1, dd, ALU.mult))
            link(dve.tensor_tensor(o1, o1, bc(w1), ALU.mult))
            link(dve.tensor_tensor(o2, o2, bc(w2), ALU.mult))
            link(dve.tensor_tensor(o1, o1, o2, ALU.add))
            link(by_group(comb, o1))
            seen(dve, ("pos",))
            b = bank(("pos",))
            pv, psrc = pos[:, :, :], b[:, 0:3 * NE].rearrange("p (t e) -> p t e", t=3)
            dve.wait_ge(member_ready, 1)
            link(dve.memset(pos[:, 2, :], 0.0))
            link(dve.scalar_tensor_tensor(out=pos[:, 0:2, :], in0=psrc[:, 0:2, :], scalar=1.0, in1=member[:, 0:2, :], op0=ALU.add, op1=ALU.mult))
            link(dve.scalar_tensor_tensor(out=pos[0:24, 2, :], in0=psrc[0:24, 2, :], scalar=1.0, in1=member[0:24, 2, :], op0=ALU.add, op1=ALU.mult))
            link(dve.tensor_scalar(pv, pv, -1.0, None, ALU.add))
            link(dve.tensor_reduce(out=most[:, 0:1], in_=b[:, 3 * NE:4 * NE], axis=AX.X, op=ALU.max))
            free(dve.memset(most[:, 1:2], 0.0))
            dve.tensor_copy(most_i[:, :], most[:, 0:1]).then_inc(pos_ready, 1)

            dve.wait_ge(mcon_in, 16)
            iota = mcon[:, MCON["iota"]:MCON["iota"] + CAP]

            def places(p, rd):
                for j in range(2):
                    e = 2 * p + j
                    if p > 0 or rd:
                        seen(dve, ("x", p - 1, 7, rd) if p else ("x", NE // 2 - 1, 7, rd - 1))
                    for tt in range(3):
                        ins = dve.tensor_scalar(G[:, tt, j, :], iota, pos[:, tt, e:e + 1], None, ALU.is_equal)
                ins.then_inc(G_ready, 1)

            def weighted(e, rd):
                if e >= 2 or rd:
                    seen(dve, ("st", (e - 2) % NE, rd if e >= 2 else rd - 1))
                for tt in range(3):
                    ins = dve.tensor_scalar(Gc[:, e % 2, tt, :], iota, pos[:, tt, e:e + 1], comb[:, tt, e:e + 1],
                                            ALU.is_equal, ALU.mult)
                ins.then_inc(Gc_ready, 1)

            def experts_dve(rd):
                base = NMIX + rd * PER_ROUND
                if rd:
                    link(dve.tensor_scalar(pv, pv, -float(CAP), None, ALU.add))
                for i in range(0 if rd else 2, LOOK):
                    lo(base + i)
                places(0, rd)
                weighted(0, rd)
                w = base
                n_e = rd * NE
                for e in range(NE + 1):
                    if e < NE:
                        if e % 2 == 0 and e // 2 + 1 < NE // 2:
                            places(e // 2 + 1, rd)
                        if e + 1 < NE:
                            weighted(e + 1, rd)
                        for _ in range(4):
                            if w + LOOK < base + PER_ROUND:
                                lo(w + LOOK)
                            w += 1
                        if e >= 2 or rd:
                            seen(dve, ("tr", (e - 2) % NE, rd if e >= 2 else rd - 1))
                        dve.wait_ge(sg2_ready, n_e + e + 1)
                        free(dve.tensor_tensor(t_f[:, e % 2, :], bank(("hg", e, rd))[:, :], sgm[:, e % 2, :], ALU.mult))
                    if e > 0:
                        dve.wait_ge(aThi_ready, n_e + e)
                        free(dve.tensor_tensor(aT_lo[:, :, :], bank(("tr", e - 1, rd))[:, :].rearrange("p (k c) -> p k c", k=4),
                                               aT_hi[:, :, :].bitcast(f32), ALU.subtract))
                    if e % YS == 1 and e > YS:
                        scattered(e // YS - 1, rd)
                    if e < NE:
                        for _ in range(4):
                            if w + LOOK < base + PER_ROUND:
                                lo(w + LOOK)
                            w += 1
                        seen(dve, ("hu", e, rd))
                        dve.wait_ge(dve_freed, TILE[("hg", e, rd)][2])
                        free(dve.tensor_tensor(t_f[:, e % 2, :], bank(("hu", e, rd))[:, :], t_f[:, e % 2, :], ALU.mult))
                    if e > 0:
                        for j in range(2):
                            for _ in range(2):
                                if w + LOOK < base + PER_ROUND:
                                    lo(w + LOOK)
                                w += 1
                            dve.wait_ge(yhi2_ready, 2 * (n_e + e - 1) + j + 1)
                            sl = slice(j * 512, (j + 1) * 512)
                            free(dve.scalar_tensor_tensor(out=Y_lo[:, (e - 1) % YS, sl], in0=bank(("dn", e - 1, j, rd))[:, :],
                                                          scalar=cslot[:, e - 1:e], in1=Y_hi[:, (e - 1) % YS, sl].bitcast(f32),
                                                          op0=ALU.mult, op1=ALU.subtract))
                scattered(NE // YS - 1, rd)

            def scattered(q, rd):
                for f in range(KT):
                    seen(dve, ("y", q, f, rd))
                    if q or rd:
                        dve.wait_ge(dve_freed, TILE[("y", q - 1, f, rd) if q else ("y", NE // YS - 1, f, rd - 1)][2])
                    free(dve.tensor_tensor(xT[:, f, :], bank(("y", q, f, rd))[:, 0:T], xT[:, f, :], ALU.add))

            experts_dve(0)
            later_rounds(dve, experts_dve)

        @block.tensor
        def _(pe):
            at = {"i": 0}

            def opened(name):
                i = TILE[name][0]
                assert i == at["i"], (name, TILES[at["i"]])
                at["i"] += 1
                if i >= BANKS:
                    evacuated(pe, TILES[i - BANKS][0])
                return banks[i % BANKS]

            def done(ins):
                ins.then_inc(tile_ready, 1)

            def passes(out, w, ks, x_hi, x_lo, k0=0, m=None, first=True, last=True):
                hi, lo = part_view(w_hi, w), part_view(w_lo, w)
                cols = slice(0, 128) if m is None else slice(m * 128, (m + 1) * 128)
                for k in range(ks):
                    for j, (a, b) in enumerate(((hi, x_hi), (hi, x_lo), (lo, x_hi))):
                        ins = pe.matmul(out, a[:, k, cols], b[:, k0 + k, :], start=first and k == 0 and j == 0,
                                        stop=last and k == ks - 1 and j == 2)
                return ins

            pe.wait_ge(con_in, 16)
            pe.wait_ge(x_in, 80)
            for tt, (t0, nt) in enumerate(TOKENS):
                for hf2 in range(2):
                    b = opened(("xt", tt, hf2))
                    for f in range(4):
                        col = (4 * hf2 + f) * 128
                        ins = pe.transpose(b[:, f * 128:f * 128 + nt], x_tok[0:nt, tt, col:col + 128], ident[0:nt, 0:nt])
                    done(ins)

            pe.wait_ge(par_in, 128)
            b = opened(("par",))
            done(pe.transpose(b[:, 0:NPAR], par_rows[:, :], ident[0:NPAR, 0:NPAR]))

            def norm_pe(i, sq):
                b = opened(("norm", i))
                for f in range(KT):
                    if f % 4 == 0:
                        pe.wait_ge(sq_ready, 2 * i + f // 4 + 1)
                    ins = pe.matmul(b[:, 0:T], cst("mean_d"), sq[:, f, :], start=f == 0, stop=f == KT - 1)
                done(ins)

            norm_pe(0, sq0)

            def samp_o(s):
                h = s // 4
                evacuated(pe, ("vb", s, 1))
                if s % 4 == 0 and h >= 1:
                    pe.wait_ge(osb_ready, h)
                for j in range(2):
                    smp = 2 * (s % 4) + j
                    for dt in range(2):
                        q = 32 * (2 * j + dt)
                        ins = pe.matmul(o_samp[q:q + NSAMP, :], qm[:, 2 * h + dt, smp, :], S_ring[:, s % 2, j, dt, :],
                                        start=s % 4 == 0, stop=s % 4 == 3)
                ins.then_inc(S_used, 1)

            for w in range(NMIX):
                s, i = UNITS[w]
                if w == 0:
                    pe.wait_ge(hlo_ready, 2)
                pe.wait_ge(lo_ready, w + 1)
                if s == "ret":
                    if i == 0:
                        pe.wait_ge(ylo_ready, ET - 1)
                    if i == 1:
                        pe.wait_ge(ylo_ready, ET)
                    if i % 2 == 0:
                        b = opened(("m", w + 1))
                        passes(b[:, 0:T], w, 8, on_hi, on_lo, last=False)
                    else:
                        done(passes(b[:, 0:T], w, 8, on_hi, on_lo, k0=8, first=False))
                else:
                    xh, xl = h_hi, h_lo
                    if s == "cout":
                        xh, xl = c_hi, c_lo
                        if i == 0:
                            pe.wait_ge(clo_ready, KT)
                    if s == "wo":
                        xh, xl = m_hi, m_lo
                        if i == 0:
                            pe.wait_ge(mlo_ready, KT)
                    b = opened(("m", w))
                    done(passes(b[:, 0:T], w, 8, xh, xl))
                if w == 1:
                    pe.wait_ge(cw_in, 16)
                    b = opened(("cw",))
                    for f in range(KT):
                        ins = pe.transpose(b[:, f * CW:(f + 1) * CW], cw_rows[:, f * 128:(f + 1) * 128], ident[0:CW, 0:CW])
                    done(ins)
                if 2 <= w < 6:
                    r, hf2 = (w - 2) // 2, w % 2
                    pe.wait_ge(sc_in, 32)
                    b = opened(("sc", r, hf2))
                    for f in range(4):
                        col = (4 * hf2 + f) * 128
                        ins = pe.transpose(b[:, f * 120:(f + 1) * 120], sc_rows[:, r, col:col + 128], ident[0:120, 0:120])
                    done(ins)
                if FIRST["v"] < w <= FIRST["v"] + 16:
                    j = w - 1 - FIRST["v"]
                    evacuated(pe, ("m", w - 1))
                    b = opened(("vt", j))
                    for tt, (t0, nt) in enumerate(TOKENS):
                        ins = pe.transpose(b[0:nt, tt * 128:tt * 128 + 128], vT[:, j % 2, t0:t0 + nt], ident)
                    done(ins)
                if GLU <= w < EXTRA_END:
                    k = w - GLU
                    if k < NH:
                        h = k
                        pe.wait_ge(rot_ready, 8)
                        b = opened(("score", h))
                        col = 0
                        for t0, nt in ((0, 128), (128, 128), (256, 16)):
                            for dt in range(2):
                                ins = pe.matmul(b[0:nt, col:col + TP - t0], kT[:, 2 * h + dt, t0:t0 + nt],
                                                qT[:, 2 * h + dt, t0:TP], start=dt == 0, stop=dt == 1)
                            col += TP - t0
                        done(ins)
                        b = opened(("kt", h, 0))
                        for tt in range(2):
                            for dt in range(2):
                                c0 = tt * DK + dt * 128
                                ins = pe.transpose(b[:, c0:c0 + 128], kT[:, 2 * h + dt, tt * 128:(tt + 1) * 128], ident)
                        done(ins)
                        b = opened(("kt", h, 1))
                        for dt in range(2):
                            ins = pe.transpose(b[0:16, dt * 128:dt * 128 + 128], kT[:, 2 * h + dt, 256:272], ident)
                        done(ins)
                    if 1 <= k <= NH:
                        h = k - 1
                        evacuated(pe, ("vt", 15))
                        evacuated(pe, ("score", h))
                        for et in range(4):
                            b = opened(("o", h, et))
                            col = 0
                            for tt, (t0, nt) in enumerate(((0, 128), (128, 128), (256, 16))):
                                e0 = h * DV + et * 128
                                ins = pe.matmul(b[:, t0:TP], v_tok[0:nt, tt, e0:e0 + 128], P[0:nt, col:col + TP - t0],
                                                start=tt == 0, stop=tt == 2)
                                col += TP - t0
                            done(ins)
                        evacuated(pe, ("kt", h, 1))
                        for dt in range(2):
                            b = opened(("S", h, dt))
                            for tt in range(3):
                                ins = pe.matmul(b[:, :], k_tok[:, h % 2, tt, dt * 128:(dt + 1) * 128],
                                                v_tok[:, tt, h * DV:(h + 1) * DV], start=tt == 0, stop=tt == 2)
                            done(ins)
                    if k == 0:
                        pe.wait_ge(qm_ready, 1)
                        evacuated(pe, ("vt", 15))
                    if k < 16:
                        h = k // 4
                        for j in range(2):
                            smp = 2 * (k % 4) + j
                            b = opened(("vb", k, j))
                            done(pe.matmul(b[:, :], ident[:, 16 + smp:17 + smp].broadcast_to([128, 128]),
                                           v_tok[:, 2, h * DV:(h + 1) * DV], start=True, stop=True))
                    if 1 <= k <= 16:
                        samp_o(k - 1)
                    if k >= 5 and (k - 5) % 4 == 0 and k <= 17:
                        h = (k - 5) // 4
                        pe.wait_ge(osb_ready, h + 1)
                        b = opened(("ot", h))
                        for et in range(4):
                            ins = pe.matmul(b[:, et * 8:et * 8 + 8], osb[:, et * 128:(et + 1) * 128], cst("quads"),
                                            start=True, stop=True)
                        done(ins)
                    if k >= 6 and (k - 6) % 4 == 0 and k <= 18:
                        h = (k - 6) // 4
                        evacuated(pe, ("ot", h))
                        b = opened(("gm", h))
                        for et in range(4):
                            ins = pe.matmul(b[:, 0:T], cst("mean_v"), oT[:, 4 * h + et, :], start=et == 0, stop=et == 3)
                        done(ins)
                    if k >= 7 and (k - 7) % 4 == 0 and k <= 19:
                        h = (k - 7) // 4
                        pe.wait_ge(osq_ready, h + 1)
                        b = opened(("gv", h))
                        for et in range(4):
                            ins = pe.matmul(b[:, 0:T], cst("mean_v"), gsq[:, et, :], start=et == 0, stop=et == 3)
                        done(ins)
                    if k in (20, 21):
                        q = k - 20
                        evacuated(pe, ("m", GRET - 1))
                        b = opened(("ut", q))
                        for f in range(4):
                            ins = pe.transpose(b[0:PAD + NSAMP, f * 128:(f + 1) * 128], u[:, 4 * q + f, TP:UW], ident)
                        done(ins)
                if w == FIRST["cout"] - 4:
                    pe.wait_ge(conv_step, KT * CW + 1)
                    b = opened(("lm",))
                    for f in range(KT):
                        ins = pe.matmul(b[:, 0:T], cst("mean_d"), conv[:, f, :], start=f == 0, stop=f == KT - 1)
                    done(ins)
                if w == FIRST["cout"] - 3:
                    pe.wait_ge(csq_ready, 1)
                    b = opened(("lv",))
                    for f in range(KT):
                        ins = pe.matmul(b[:, 0:T], cst("mean_d"), ln_sq[:, f, :], start=f == 0, stop=f == KT - 1)
                    done(ins)

            norm_pe(1, sq1)
            pe.wait_ge(wr_in, 64)
            b = opened(("logit",))
            for f in range(KT):
                pe.wait_ge(h_ready, 2 + f + 1)
                ins = pe.matmul(b[0:20, 0:T], wr[:, f, :], h2f[:, f, :], start=f == 0, stop=f == KT - 1)
            done(ins)
            for tt, (t0, nt) in enumerate(TOKENS):
                for hf2 in range(2):
                    b = opened(("ht", tt, hf2))
                    for f in range(4):
                        ins = pe.transpose(b[0:nt, f * 128:(f + 1) * 128], h2f[:, 4 * hf2 + f, t0:t0 + nt], ident)
                    done(ins)
            evacuated(pe, ("logit",))
            b = opened(("lt",))
            for tt, (t0, nt) in enumerate(TOKENS):
                ins = pe.transpose(b[0:nt, tt * 20:tt * 20 + 20], lgT[:, t0:t0 + nt], ident[0:20, 0:20])
            done(ins)
            pe.wait_ge(member_ready, 1)
            pe.wait_ge(mcon_in, 16)
            b = opened(("pos",))
            before, ones = mcon[:, MCON["before"]:MCON["before"] + 128], mcon[:, MCON["ones"]:MCON["ones"] + 128]
            for tt, (_, nt) in enumerate(TOKENS):
                for k in range(tt + 1):
                    nk = TOKENS[k][1]
                    lhs = before if k == tt else ones
                    pe.matmul(b[0:nt, tt * NE:(tt + 1) * NE], lhs[0:nk, 0:nt], member[0:nk, k, :], start=k == 0, stop=k == tt)
            for k, (_, nk) in enumerate(TOKENS):
                ins = pe.matmul(b[:, 3 * NE:4 * NE], ones[0:nk, :], member[0:nk, k, :], start=k == 0, stop=k == 2)
            done(ins)

            def gather(p, js, rd):
                pe.wait_ge(G_ready, rd * NE // 2 + p + 1)
                for j in js:
                    b = opened(("x", p, j, rd))
                    src = h2t_hi if j < 4 else h2t_lo
                    for k in range(2):
                        f = 2 * (j % 4) + k
                        for tt, (_, nt) in enumerate(TOKENS):
                            ins = pe.matmul(b[:, k * 256:(k + 1) * 256], src[:, tt, f * 128:(f + 1) * 128],
                                            G[:, tt, :, :].rearrange("p e c -> p (e c)"), start=tt == 0, stop=tt == 2)
                    done(ins)

            def stream(out, w, k0, xh, xl, n_k):
                pe.wait_ge(lo_ready, w + 1)
                hi, lo = part_view(w_hi, w), part_view(w_lo, w)
                for k in range(2):
                    for j, (a, b) in enumerate(((xh, hi), (xl, hi), (xh, lo))):
                        ins = pe.matmul(out, a[:, k0 + k, :], b[:, k, :], start=k0 + k == 0 and j == 0,
                                        stop=k0 + k == n_k - 1 and j == 2)
                if w in UNIT_MID:
                    ins.then_inc(unit_mid, 1)
                return ins

            def scatter(q, rd):
                evacuated(pe, ("dn", YS * q + YS - 1, 1, rd))
                evacuated(pe, ("st", YS * q + YS - 1, rd))
                for f in range(KT):
                    b = opened(("y", q, f, rd))
                    for i in range(YS):
                        for j, src in enumerate((Y_hi, Y_lo)):
                            ins = pe.matmul(b[:, 0:T], src[:, i, f * 128:(f + 1) * 128], S_b[:, (YS * q + i) % (2 * YS), :],
                                            start=i == 0 and j == 0, stop=i == YS - 1 and j == 1)
                    done(ins)

            def experts_pe(rd):
                n_e = rd * NE
                gather(0, range(8), rd)
                for e in range(NE + 1):
                    p = e // 2
                    if e < NE:
                        evacuated(pe, ("x", p, 7, rd))
                        b = opened(("hg", e, rd))
                        for i in range(4):
                            ins = stream(b[:, :], UNIT[("g", e, i, rd)], 2 * i, x_hi[p % 2][:, e % 2], x_lo[p % 2][:, e % 2], KT)
                        done(ins)
                    if e > 0:
                        evacuated(pe, ("hu", e - 1, rd))
                        b = opened(("tr", e - 1, rd))
                        for k in range(4):
                            ins = pe.transpose(b[:, k * 128:(k + 1) * 128], t_f[:, (e - 1) % 2, k * 128:(k + 1) * 128], ident)
                        done(ins)
                    if e < NE:
                        pe.wait_ge(Gc_ready, n_e + e + 1)
                        b = opened(("st", e, rd))
                        for tt, (t0, nt) in enumerate(TOKENS):
                            ins = pe.transpose(b[:, t0:t0 + nt], Gc[0:nt, e % 2, tt, :], ident[0:nt, 0:nt])
                        done(ins)
                        if p + 1 < NE // 2:
                            gather(p + 1, range(4 * (e % 2), 4 * (e % 2) + 4), rd)
                    if e % YS == 1 and e > YS:
                        scatter(e // YS - 1, rd)
                    if e < NE:
                        b = opened(("hu", e, rd))
                        for i in range(4):
                            ins = stream(b[:, :], UNIT[("u", e, i, rd)], 2 * i, x_hi[p % 2][:, e % 2], x_lo[p % 2][:, e % 2], KT)
                        done(ins)
                    if e > 0:
                        evacuated(pe, ("tr", e - 1, rd))
                        for j in range(2):
                            b = opened(("dn", e - 1, j, rd))
                            for i in range(2):
                                ins = stream(b[:, :], UNIT[("d", e - 1, 2 * j + i, rd)], 2 * i, aT_hi, aT_lo, 4)
                            done(ins)
                scatter(NE // YS - 1, rd)

            experts_pe(0)
            dve_is_done(pe)
            later_rounds(pe, experts_pe)

        block_1.__exit__(None, None, None)

        with nc.Block() as block_2:
            fin_banks = {("yt", tt, hf2): 1 + 2 * tt + hf2 for tt in range(3) for hf2 in range(2)}

            @block_2.scalar
            def _(act):
                for k in range(2):
                    act.activation(sq2[:, 4 * k:4 * k + 4, :], xT[:, 4 * k:4 * k + 4, :], ACT.Square).then_inc(fin_sq, 1)
                act.wait_ge(fin_tile, 1)
                act.activation(rstd[:, :], banks[0][:, 0:T], ACT.Sqrt, bias=eps).then_inc(fin_std, 1)
                for tt, (t0, nt) in enumerate(TOKENS):
                    act.wait_ge(fin_tile, 2 + 2 * tt)
                    act.activation(y_tok[0:nt, tt, 0:512], banks[fin_banks[("yt", tt, 0)]][0:nt, :], ACT.Copy).then_inc(fin_act, 1)

            @block_2.vector
            def _(dve):
                dve.wait_ge(fin_std, 1)
                dve.reciprocal(rstd[:, :], rstd[:, :]).then_inc(fin_std, 1)
                dve.wait_ge(fin_std, 2)
                for f in range(KT):
                    g = par[:, PAR["norm_final"] + f:PAR["norm_final"] + f + 1]
                    dve.scalar_tensor_tensor(out=hfin[:, f, :], in0=xT[:, f, :], scalar=g, in1=rstd[:, :],
                                             op0=ALU.mult, op1=ALU.mult).then_inc(fin_h, 1)
                for tt, (t0, nt) in enumerate(TOKENS):
                    dve.wait_ge(fin_tile, 3 + 2 * tt)
                    dve.tensor_copy(y_tok[0:nt, tt, 512:1024], banks[fin_banks[("yt", tt, 1)]][0:nt, :]).then_inc(fin_dve, 1)

            @block_2.tensor
            def _(pe):
                for f in range(KT):
                    pe.wait_ge(fin_sq, f // 4 + 1)
                    ins = pe.matmul(banks[0][:, 0:T], cst("mean_d"), sq2[:, f, :], start=f == 0, stop=f == KT - 1)
                ins.then_inc(fin_tile, 1)
                for tt, (t0, nt) in enumerate(TOKENS):
                    for hf2 in range(2):
                        b = banks[fin_banks[("yt", tt, hf2)]]
                        for f in range(4):
                            pe.wait_ge(fin_h, 4 * hf2 + f + 1)
                            ins = pe.transpose(b[0:nt, f * 128:(f + 1) * 128], hfin[:, 4 * hf2 + f, t0:t0 + nt], ident)
                        ins.then_inc(fin_tile, 1)

            @block_2.sync
            def _(sp):
                n1 = 128 - NMETA
                sp.wait_ge(fin_act, 1)
                sp.wait_ge(fin_dve, 1)
                sp.dma_start(O["y_prompt"][0, 0:n1], y_tok[NMETA:128, 0, :]).then_inc(y_stored, 16)
                sp.wait_ge(fin_act, 2)
                sp.wait_ge(fin_dve, 2)
                sp.dma_start(O["y_prompt"][0, n1:n1 + 128], y_tok[:, 1, :]).then_inc(y_stored, 16)
                sp.wait_ge(fin_act, 3)
                sp.wait_ge(fin_dve, 3)
                sp.dma_start(O["y_prompt"][0, n1 + 128:SEQ], y_tok[0:16, 2, :]).then_inc(y_stored, 16)
                sp.dma_start(O["y_sample"][:, 0, :], y_tok[16:24, 2, :]).then_inc(y_stored, 16)
                sp.wait_ge(y_stored, 16 * 4)
                sp.wait_ge(rows_stored, 16 * 3)
                for i in range(2):
                    sp.wait_ge(S_stored[i], 16 * 16)
                    sp.wait_ge(Sp_stored[i], 16 * NH)


def hg_before(e, rd):
    return ("hg", (e - 2) % NE, rd if e >= 2 else rd - 1)


_INS = ["x_prompt", "x_sample", "state_ret", "state_conv", "meta_tokens", "norm_mix_g", "w_in", "b_gates", "conv_w",
        "conv_b", "conv_ln_g", "conv_ln_b", "w_conv_out", "ret_gn_g", "w_ret_out", "w_o", "norm_ffn_g", "w_coarse",
        "b_coarse", "w_fine", "b_fine", "w_gate_e", "w_up_e", "w_down_e", "norm_final_g"]
_OUTS = [("y_prompt", (1, SEQ, D)), ("y_sample", (NSAMP, 1, D)), ("ret_prompt", (1, 1, NH, DK, DV)),
         ("conv_prompt", (1, 1, PAD, D)), ("ret_sample", (1, NSAMP, NH, DK, DV)), ("conv_sample", (1, NSAMP, PAD, D))]


def kernel(**inputs):
    import numpy as _np
    import concourse.bacc as _bacc
    from concourse import mybir as _mybir
    from concourse.bass_utils import run_bass_kernel_spmd as _run

    nc = _bacc.Bacc("TRN2", target_bir_lowering=False, num_devices=1)
    arrays, A, O = {}, {}, {}
    for name in _INS:
        a = _np.ascontiguousarray(inputs[name])
        arrays[f"in_{name}"] = a
        A[name] = nc.dram_tensor(f"in_{name}", a.shape, _mybir.dt.from_np(a.dtype), kind="ExternalInput").ap()
    c = constants()
    arrays["constants"] = c
    C = nc.dram_tensor("constants", c.shape, _mybir.dt.from_np(c.dtype), kind="ExternalInput").ap()
    for name, shape in _OUTS:
        O[name] = nc.dram_tensor(f"out_{name}", shape, _mybir.dt.float32, kind="ExternalOutput").ap()
    c2 = moe_constants()
    arrays["moe_constants"] = c2
    C2 = nc.dram_tensor("moe_constants", c2.shape, _mybir.dt.from_np(c2.dtype), kind="ExternalInput").ap()
    build(nc, A, C, C2, O)
    r = _run(nc, [arrays], core_ids=[0])
    return tuple(r.results[0][f"out_{name}"] for name, _ in _OUTS)
```
